# Optimizing a Trainium2 kernel written in Bass

```python
import jax, jax.numpy as jnp
from jax import lax
import numpy as np

D_MODEL = 2048
BATCH = 1
SEQ = 256
DEPTH = 1

CHUNK = 64
H_A = 8
DK_A = 128
DV_A = 128
D_A = H_A * DK_A
H_B = 8
DH_B = 128
D_B = H_B * DH_B
N_PAST_CHUNKS = 8
BAND = N_PAST_CHUNKS + 1
REL_FUTURE = CHUNK - 1
REL_PAST = 2 * CHUNK - 1
N_REL = REL_FUTURE + REL_PAST + 1
D_FF = -(-8 * D_MODEL // (3 * 256)) * 256
N_IN = 4 * D_A + 3 * D_B + 2 * D_MODEL
EPS = 1e-6


def rms_norm(x, gain):
    xf = x.astype(jnp.float32)
    y = xf * lax.rsqrt(jnp.mean(xf * xf, axis=-1, keepdims=True) + EPS)
    return (y * gain.astype(jnp.float32)).astype(x.dtype)

def hgrn_lower_bounds(lb_logits):
    p = jax.nn.softmax(lb_logits.astype(jnp.float32), axis=0)
    return jnp.cumsum(p, axis=0)[:DEPTH]

def hgrn2_mixer(q, f_logit, i, g, lb, out_gain):
    B, T, _ = q.shape
    n_chunks = T // CHUNK
    f32 = jnp.float32
    lbf = lb.astype(f32)
    f = lbf + (1.0 - lbf) * jax.nn.sigmoid(f_logit.astype(f32))
    log_f = jnp.log(f)
    k = 1.0 - f
    qs = jax.nn.silu(q.astype(f32))

    def to_chunks(t, dh):
        return t.reshape(B, n_chunks, CHUNK, H_A, dh).transpose(1, 0, 3, 2, 4)

    qc, kc, lfc = to_chunks(qs, DK_A), to_chunks(k, DK_A), to_chunks(log_f, DK_A)
    vc = to_chunks(i.astype(f32), DV_A)
    causal = jnp.tril(jnp.ones((CHUNK, CHUNK), dtype=bool))[:, :, None]

    def step(S, inp):
        qj, kj, lfj, vj = inp
        b = jnp.cumsum(lfj, axis=2)
        o_inter = jnp.einsum('bhtk,bhkv->bhtv', qj * jnp.exp(b), S)
        rel = jnp.where(causal, b[:, :, :, None, :] - b[:, :, None, :, :], -jnp.inf)
        decay = jnp.exp(rel)
        scores = jnp.einsum('bhtk,bhsk,bhtsk->bhts', qj, kj, decay)
        o_intra = jnp.einsum('bhts,bhsv->bhtv', scores, vj)
        b_last = b[:, :, -1:, :]
        S_new = jnp.exp(b_last[:, :, 0, :, None]) * S + jnp.einsum(
            'bhsk,bhsv->bhkv', kj * jnp.exp(b_last - b), vj)
        return S_new, o_inter + o_intra

    S0 = jnp.zeros((B, H_A, DK_A, DV_A), f32)
    _, o = lax.scan(step, S0, (qc, kc, lfc, vc))
    o = o.transpose(1, 0, 3, 2, 4).reshape(B, T, H_A, DV_A)
    o = o * lax.rsqrt(jnp.mean(o * o, axis=-1, keepdims=True) + EPS)
    o = o.reshape(B, T, D_A) * out_gain.astype(f32)
    o = o * jax.nn.silu(g.astype(f32))
    return o.astype(q.dtype)

def head_rms_norm(t, gain):
    tf = t.astype(jnp.float32)
    y = tf * lax.rsqrt(jnp.mean(tf * tf, axis=-1, keepdims=True) + EPS)
    return y * gain.astype(jnp.float32)

def chunked_relpos_attention(q, k, v, q_gain, k_gain, rel_bias):
    B, T, _ = q.shape
    n_chunks = T // CHUNK

    def heads(t):
        return t.reshape(B, n_chunks, CHUNK, H_B, DH_B).transpose(0, 3, 1, 2, 4)

    qh = head_rms_norm(heads(q), q_gain)
    kh = head_rms_norm(heads(k), k_gain)
    vh = heads(v).astype(jnp.float32)

    pad = ((0, 0), (0, 0), (N_PAST_CHUNKS, 0), (0, 0), (0, 0))
    band_idx = jnp.arange(n_chunks)[:, None] + jnp.arange(BAND)[None, :]
    k_band = jnp.pad(kh, pad)[:, :, band_idx].reshape(B, H_B, n_chunks, BAND * CHUNK, DH_B)
    v_band = jnp.pad(vh, pad)[:, :, band_idx].reshape(B, H_B, n_chunks, BAND * CHUNK, DH_B)

    q_pos = jnp.arange(n_chunks)[:, None] * CHUNK + jnp.arange(CHUNK)[None, :]
    k_chunk = band_idx - N_PAST_CHUNKS
    k_pos = (k_chunk[:, :, None] * CHUNK + jnp.arange(CHUNK)[None, None, :]).reshape(
        n_chunks, BAND * CHUNK)
    valid = k_pos >= 0
    dist = q_pos[:, :, None] - k_pos[:, None, :]
    rel_idx = jnp.clip(dist, -REL_FUTURE, REL_PAST) + REL_FUTURE
    bias = rel_bias.astype(jnp.float32)[:, rel_idx]

    scale = DH_B ** -0.5
    scores = jnp.einsum('bhnqd,bhnkd->bhnqk', qh, k_band) * scale + bias[None]
    scores = jnp.where(valid[None, None, :, None, :], scores, -jnp.inf)
    p = jax.nn.softmax(scores, axis=-1)
    o = jnp.einsum('bhnqk,bhnkd->bhnqd', p, v_band)
    return o.transpose(0, 2, 3, 1, 4).reshape(B, T, D_B).astype(q.dtype)

def first_inputs(seed: int = 0) -> dict:
    key = jax.random.key(seed)
    ks = jax.random.split(key, 16)
    f32 = jnp.float32

    def nrm(k, shape, scale):
        return jax.random.normal(k, shape, f32) * scale

    return {
        "x": nrm(ks[0], (BATCH, SEQ, D_MODEL), 1.0),
        "w_in": nrm(ks[1], (DEPTH, D_MODEL, N_IN), D_MODEL ** -0.5),
        "b_gate": nrm(ks[2], (DEPTH, 2 * D_MODEL), 0.02),
        "norm_mix": 1.0 + nrm(ks[3], (DEPTH, D_MODEL), 0.02),
        "norm_ffn": 1.0 + nrm(ks[4], (DEPTH, D_MODEL), 0.02),
        "hgrn_lb_logits": nrm(ks[5], (DEPTH + 1, D_A), 0.5),
        "hgrn_out_gain": 1.0 + nrm(ks[6], (DEPTH, D_A), 0.02),
        "q_gain": 1.0 + nrm(ks[7], (DEPTH, DH_B), 0.02),
        "k_gain": 1.0 + nrm(ks[8], (DEPTH, DH_B), 0.02),
        "rel_bias": nrm(ks[9], (DEPTH, H_B, N_REL), 0.1),
        "w_proj_a": nrm(ks[10], (DEPTH, D_A, D_MODEL), D_A ** -0.5),
        "w_proj_b": nrm(ks[11], (DEPTH, D_B, D_MODEL), D_B ** -0.5),
        "w_out": nrm(ks[12], (DEPTH, D_MODEL, D_MODEL), D_MODEL ** -0.5),
        "w_ffn_in": nrm(ks[13], (DEPTH, D_MODEL, 2 * D_FF), D_MODEL ** -0.5),
        "w_ffn_out": nrm(ks[14], (DEPTH, D_FF, D_MODEL), D_FF ** -0.5),
    }

def first_block(x, w_in, b_gate, norm_mix, norm_ffn, hgrn_lb_logits, hgrn_out_gain,
              q_gain, k_gain, rel_bias, w_proj_a, w_proj_b, w_out, w_ffn_in, w_ffn_out):
    lower_bounds = hgrn_lower_bounds(hgrn_lb_logits)
    split_pts = [D_A, 2 * D_A, 3 * D_A, 4 * D_A,
                 4 * D_A + D_B, 4 * D_A + 2 * D_B, 4 * D_A + 3 * D_B]
    for l in range(DEPTH):
        h = rms_norm(x, norm_mix[l])
        proj = jnp.einsum('btd,dn->btn', h, w_in[l])
        q_a, f_a, i_a, g_a, q_b, k_b, v_b, gate_logits = jnp.split(proj, split_pts, axis=-1)
        gates = jax.nn.sigmoid((gate_logits + b_gate[l]).astype(jnp.float32)).astype(x.dtype)
        gate_a, gate_b = jnp.split(gates, 2, axis=-1)

        y_a = hgrn2_mixer(q_a, f_a, i_a, g_a, lower_bounds[l], hgrn_out_gain[l])
        y_b = chunked_relpos_attention(q_b, k_b, v_b, q_gain[l], k_gain[l], rel_bias[l])

        merged = (gate_a * jnp.einsum('btc,cd->btd', y_a, w_proj_a[l])
                  + gate_b * jnp.einsum('btc,cd->btd', y_b, w_proj_b[l]))
        x = x + jnp.einsum('btd,de->bte', merged, w_out[l])

        h = rms_norm(x, norm_ffn[l])
        gate_up = jnp.einsum('btd,df->btf', h, w_ffn_in[l])
        ff_gate, ff_up = jnp.split(gate_up, 2, axis=-1)
        x = x + jnp.einsum('btf,fd->btd', jax.nn.silu(ff_gate) * ff_up, w_ffn_out[l])
    return x


HEAD_DIM = 128
MIX_WIDTH = D_MODEL
NSA_HEADS = MIX_WIDTH // 2 // HEAD_DIM
NSA_KV_GROUPS = 2
NSA_HPG = NSA_HEADS // NSA_KV_GROUPS
MOBA_HEADS = MIX_WIDTH // 2 // HEAD_DIM
CMP_LEN = 32
CMP_STRIDE = 16
CMP_HIDDEN = HEAD_DIM
SEL_LEN = 64
SEL_TOPK = 16
WINDOW = 512
MOBA_BLOCK = 256
MOBA_TOPK = 3
D_FF_2 = 4 * D_MODEL
ROPE_THETA = 10000.0
NSA_Q_CHUNK = 64
MOBA_Q_CHUNK = 16

NSA_Q_W = NSA_HEADS * HEAD_DIM
NSA_KV_W = NSA_KV_GROUPS * HEAD_DIM
NSA_GATE_W = 3 * NSA_HEADS
MOBA_W = MOBA_HEADS * HEAD_DIM
IN_WIDTHS = (NSA_Q_W,) + (NSA_KV_W,) * 6 + (NSA_GATE_W, MOBA_W, MOBA_W, MOBA_W)
IN_COLS = sum(IN_WIDTHS)


def rms_norm_2(x, g):
    x32 = x.astype(jnp.float32)
    y = x32 * lax.rsqrt(jnp.mean(x32 * x32, axis=-1, keepdims=True) + EPS)
    return (y * g.astype(jnp.float32)).astype(x.dtype)

def modulate(h, shift, scale):
    return h * (1.0 + scale[:, None, :]) + shift[:, None, :]

def rope_tables(T):
    pos = jnp.arange(T, dtype=jnp.float32)
    inv = ROPE_THETA ** (-jnp.arange(0, HEAD_DIM, 2, dtype=jnp.float32) / HEAD_DIM)
    ang = pos[:, None] * inv[None, :]
    return jnp.cos(ang), jnp.sin(ang)

def apply_rope(x, cos, sin):
    shp = (x.shape[1],) + (1,) * (x.ndim - 3) + (HEAD_DIM // 2,)
    c_ = cos.reshape(shp)
    s_ = sin.reshape(shp)
    x32 = x.astype(jnp.float32)
    x1, x2 = jnp.split(x32, 2, axis=-1)
    return jnp.concatenate([x1 * c_ - x2 * s_, x2 * c_ + x1 * s_], axis=-1).astype(x.dtype)

def masked_softmax(s, mask):
    s = jnp.where(mask, s.astype(jnp.float32), -jnp.inf)
    m = jnp.max(s, axis=-1, keepdims=True)
    m = jnp.where(jnp.isfinite(m), m, 0.0)
    e = jnp.exp(s - m)
    return e / jnp.maximum(jnp.sum(e, axis=-1, keepdims=True), jnp.float32(1e-30))

def compress(x, pos, w1, w2):
    B, T, G, dh = x.shape
    n_cmp = (T - CMP_LEN) // CMP_STRIDE + 1
    idx = np.arange(n_cmp)[:, None] * CMP_STRIDE + np.arange(CMP_LEN)[None, :]
    blocks = x[:, idx] + pos[:, None, :].astype(x.dtype)
    blocks = blocks.transpose(0, 1, 3, 2, 4).reshape(B, n_cmp, G, CMP_LEN * dh)
    return jax.nn.silu(blocks @ w1) @ w2

def nsa_mixer(q, k_cmp, v_cmp, k_sel, v_sel, k_win, v_win, gate_logits,
              cmp_k_pos, cmp_k_w1, cmp_k_w2, cmp_v_pos, cmp_v_w1, cmp_v_w2, cos, sin):
    B, T, _ = q.shape
    G, Hg, dh = NSA_KV_GROUPS, NSA_HPG, HEAD_DIM
    Qc = NSA_Q_CHUNK
    q = apply_rope(q.reshape(B, T, G, Hg, dh), cos, sin) * (dh ** -0.5)
    kv = lambda a: a.reshape(B, T, G, dh)
    k_cmp = apply_rope(kv(k_cmp), cos, sin)
    k_sel = apply_rope(kv(k_sel), cos, sin)
    k_win = apply_rope(kv(k_win), cos, sin)
    v_cmp, v_sel, v_win = kv(v_cmp), kv(v_sel), kv(v_win)
    gates = jax.nn.sigmoid(gate_logits.astype(jnp.float32)).reshape(B, T, G, Hg, 3)

    kc = compress(k_cmp, cmp_k_pos, cmp_k_w1, cmp_k_w2)
    vc = compress(v_cmp, cmp_v_pos, cmp_v_w1, cmp_v_w2)
    n_cmp = kc.shape[1]
    cmp_start = np.arange(n_cmp) * CMP_STRIDE
    cmp_end_np = cmp_start + CMP_LEN
    cmp_end = jnp.asarray(cmp_end_np - 1)

    n_sel = T // SEL_LEN
    k_top = min(SEL_TOPK, n_sel)
    sel_start = np.arange(n_sel) * SEL_LEN
    overlap = np.clip(np.minimum(cmp_end_np[:, None], sel_start[None, :] + SEL_LEN)
                      - np.maximum(cmp_start[:, None], sel_start[None, :]), 0, None)
    sel_map = jnp.asarray((overlap / CMP_LEN).astype(np.float32))
    ks_blk = k_sel.reshape(B, n_sel, SEL_LEN, G, dh).transpose(0, 3, 1, 2, 4)
    vs_blk = v_sel.reshape(B, n_sel, SEL_LEN, G, dh).transpose(0, 3, 1, 2, 4)
    bi = jnp.arange(B)[:, None, None, None]
    gi = jnp.arange(G)[None, :, None, None]

    pad = ((0, 0), (WINDOW, 0), (0, 0), (0, 0))
    kw_pad = jnp.pad(k_win, pad)
    vw_pad = jnp.pad(v_win, pad)

    def chunk(i):
        s0 = i * Qc
        qc = lax.dynamic_slice_in_dim(q, s0, Qc, axis=1)
        gc = lax.dynamic_slice_in_dim(gates, s0, Qc, axis=1)
        tq = s0 + jnp.arange(Qc)
        sc = jnp.einsum('bqghd,bcgd->bghqc', qc, kc)
        p_c = masked_softmax(sc, cmp_end[None, :] <= tq[:, None])
        o_c = jnp.einsum('bghqc,bcgd->bqghd', p_c.astype(vc.dtype), vc)
        imp = jnp.einsum('bghqc,cs->bgqs', p_c, sel_map)
        cb = tq // SEL_LEN
        blk = jnp.arange(n_sel)[None, :]
        causal = blk <= cb[:, None]
        forced = (blk == 0) | (blk == cb[:, None]) | (blk == cb[:, None] - 1)
        score = jnp.where(causal, jnp.where(forced, jnp.inf, imp), -jnp.inf)
        _, idx = lax.top_k(score, k_top)
        ksg = ks_blk[bi, gi, idx]
        vsg = vs_blk[bi, gi, idx]
        kpos = idx[..., None] * SEL_LEN + jnp.arange(SEL_LEN)
        mask_s = (kpos <= tq[:, None, None]).reshape(B, G, 1, Qc, k_top * SEL_LEN)
        ss = jnp.einsum('bqghd,bgqkld->bghqkl', qc, ksg).reshape(B, G, Hg, Qc, k_top * SEL_LEN)
        p_s = masked_softmax(ss, mask_s)
        o_s = jnp.einsum('bghqn,bgqnd->bqghd', p_s.astype(vsg.dtype),
                         vsg.reshape(B, G, Qc, k_top * SEL_LEN, dh))
        kw = lax.dynamic_slice_in_dim(kw_pad, s0, Qc + WINDOW, axis=1)
        vw = lax.dynamic_slice_in_dim(vw_pad, s0, Qc + WINDOW, axis=1)
        kp = s0 - WINDOW + jnp.arange(Qc + WINDOW)
        dist = tq[:, None] - kp[None, :]
        mask_w = (dist >= 0) & (dist < WINDOW) & (kp[None, :] >= 0)
        sw = jnp.einsum('bqghd,bkgd->bghqk', qc, kw)
        p_w = masked_softmax(sw, mask_w)
        o_w = jnp.einsum('bghqk,bkgd->bqghd', p_w.astype(vw.dtype), vw)
        g = gc.astype(o_c.dtype)
        o = g[..., 0:1] * o_c + g[..., 1:2] * o_s + g[..., 2:3] * o_w
        return o.reshape(B, Qc, NSA_HEADS * dh)

    out = lax.map(chunk, jnp.arange(T // Qc))
    return jnp.moveaxis(out, 0, 1).reshape(B, T, NSA_HEADS * dh)

def moba_mixer(q, k, v, cos, sin):
    B, T, _ = q.shape
    H, dh, BLK, Qc = MOBA_HEADS, HEAD_DIM, MOBA_BLOCK, MOBA_Q_CHUNK
    q = apply_rope(q.reshape(B, T, H, dh), cos, sin) * (dh ** -0.5)
    k = apply_rope(k.reshape(B, T, H, dh), cos, sin)
    v = v.reshape(B, T, H, dh)
    nb = -(-T // BLK)
    pad = ((0, 0), (0, nb * BLK - T), (0, 0), (0, 0))
    k_pad = jnp.pad(k, pad)
    v_pad = jnp.pad(v, pad)
    k_blk = k_pad.reshape(B, nb, BLK, H, dh).transpose(0, 3, 1, 2, 4)
    v_blk = v_pad.reshape(B, nb, BLK, H, dh).transpose(0, 3, 1, 2, 4)
    k_mean = jnp.mean(k_blk.astype(jnp.float32), axis=3).astype(k.dtype)
    k_past = min(MOBA_TOPK, nb - 1)
    bi = jnp.arange(B)[:, None, None, None]
    hi = jnp.arange(H)[None, :, None, None]

    def chunk(i):
        s0 = i * Qc
        qc = lax.dynamic_slice_in_dim(q, s0, Qc, axis=1)
        tq = s0 + jnp.arange(Qc)
        cur = s0 // BLK
        ko = lax.dynamic_slice_in_dim(k_pad, cur * BLK, BLK, axis=1)
        vo = lax.dynamic_slice_in_dim(v_pad, cur * BLK, BLK, axis=1)
        opos = cur * BLK + jnp.arange(BLK)
        s_own = jnp.einsum('bqhd,blhd->bhql', qc, ko)
        m_own = jnp.broadcast_to(opos[None, :] <= tq[:, None], (B, H, Qc, BLK))
        if k_past > 0:
            gsc = jnp.einsum('bqhd,bhnd->bhqn', qc, k_mean).astype(jnp.float32)
            gsc = jnp.where(jnp.arange(nb) < cur, gsc, -jnp.inf)
            _, idx = lax.top_k(gsc, k_past)
            kg = k_blk[bi, hi, idx]
            vg = v_blk[bi, hi, idx]
            s_past = jnp.einsum('bqhd,bhqkld->bhqkl', qc, kg).reshape(B, H, Qc, k_past * BLK)
            m_past = jnp.broadcast_to((idx < cur)[..., None],
                                      (B, H, Qc, k_past, BLK)).reshape(B, H, Qc, k_past * BLK)
            p = masked_softmax(jnp.concatenate([s_past, s_own], axis=-1),
                               jnp.concatenate([m_past, m_own], axis=-1))
            p = p.astype(v.dtype)
            o = (jnp.einsum('bhqn,bhqnd->bqhd', p[..., :k_past * BLK],
                            vg.reshape(B, H, Qc, k_past * BLK, dh))
                 + jnp.einsum('bhql,blhd->bqhd', p[..., k_past * BLK:], vo))
        else:
            p = masked_softmax(s_own, m_own).astype(v.dtype)
            o = jnp.einsum('bhql,blhd->bqhd', p, vo)
        return o.reshape(B, Qc, H * dh)

    out = lax.map(chunk, jnp.arange(T // Qc))
    return jnp.moveaxis(out, 0, 1).reshape(B, T, H * dh)

def second_inputs(seed: int = 0) -> dict:
    key = jax.random.key(seed)
    ks = jax.random.split(key, 18)
    nrm = lambda k, shape, s: jax.random.normal(k, shape, jnp.float32) * s
    L = DEPTH
    return {
        'x': nrm(ks[0], (BATCH, SEQ, D_MODEL), 1.0),
        'c': nrm(ks[1], (BATCH, D_MODEL), 1.0),
        'w_ada': nrm(ks[2], (L, D_MODEL, 6 * D_MODEL), 0.5 * D_MODEL ** -0.5),
        'b_ada': nrm(ks[3], (L, 6 * D_MODEL), 0.01),
        'pre_norm_mix': 1.0 + nrm(ks[4], (L, D_MODEL), 0.05),
        'post_norm_mix': 1.0 + nrm(ks[5], (L, D_MODEL), 0.05),
        'w_in': nrm(ks[6], (L, D_MODEL, IN_COLS), D_MODEL ** -0.5),
        'cmp_k_pos': nrm(ks[7], (L, CMP_LEN, HEAD_DIM), 0.1),
        'cmp_k_w1': nrm(ks[8], (L, CMP_LEN * HEAD_DIM, CMP_HIDDEN), (CMP_LEN * HEAD_DIM) ** -0.5),
        'cmp_k_w2': nrm(ks[9], (L, CMP_HIDDEN, HEAD_DIM), CMP_HIDDEN ** -0.5),
        'cmp_v_pos': nrm(ks[10], (L, CMP_LEN, HEAD_DIM), 0.1),
        'cmp_v_w1': nrm(ks[11], (L, CMP_LEN * HEAD_DIM, CMP_HIDDEN), (CMP_LEN * HEAD_DIM) ** -0.5),
        'cmp_v_w2': nrm(ks[12], (L, CMP_HIDDEN, HEAD_DIM), CMP_HIDDEN ** -0.5),
        'w_o': nrm(ks[13], (L, MIX_WIDTH, D_MODEL), MIX_WIDTH ** -0.5),
        'pre_norm_ffn': 1.0 + nrm(ks[14], (L, D_MODEL), 0.05),
        'post_norm_ffn': 1.0 + nrm(ks[15], (L, D_MODEL), 0.05),
        'w_up': nrm(ks[16], (L, D_MODEL, D_FF_2), D_MODEL ** -0.5),
        'w_down': nrm(ks[17], (L, D_FF_2, D_MODEL), D_FF_2 ** -0.5),
    }

def second_block(x, c, w_ada, b_ada, pre_norm_mix, post_norm_mix, w_in,
              cmp_k_pos, cmp_k_w1, cmp_k_w2, cmp_v_pos, cmp_v_w1, cmp_v_w2,
              w_o, pre_norm_ffn, post_norm_ffn, w_up, w_down):
    T = x.shape[1]
    cos, sin = rope_tables(T)
    split_at = np.cumsum(IN_WIDTHS)[:-1].tolist()
    for l in range(DEPTH):
        mod = jax.nn.silu(c) @ w_ada[l] + b_ada[l]
        shift_m, scale_m, gate_m, shift_f, scale_f, gate_f = jnp.split(mod, 6, axis=-1)
        h = modulate(rms_norm_2(x, pre_norm_mix[l]), shift_m, scale_m)
        (q_n, k_c, v_c, k_s, v_s, k_w, v_w, g_n,
         q_m, k_m, v_m) = jnp.split(h @ w_in[l], split_at, axis=-1)
        o_n = nsa_mixer(q_n, k_c, v_c, k_s, v_s, k_w, v_w, g_n,
                        cmp_k_pos[l], cmp_k_w1[l], cmp_k_w2[l],
                        cmp_v_pos[l], cmp_v_w1[l], cmp_v_w2[l], cos, sin)
        o_m = moba_mixer(q_m, k_m, v_m, cos, sin)
        o = jnp.concatenate([o_n, o_m], axis=-1) @ w_o[l]
        x = x + gate_m[:, None, :] * rms_norm_2(o, post_norm_mix[l])
        h = modulate(rms_norm_2(x, pre_norm_ffn[l]), shift_f, scale_f)
        f = jnp.square(jax.nn.relu(h @ w_up[l])) @ w_down[l]
        x = x + gate_f[:, None, :] * rms_norm_2(f, post_norm_ffn[l])
    return x


def setup_inputs(seed=0):
    out = dict(first_inputs(seed))
    for name, value in second_inputs(seed + 1).items():
        if name != "x":
            out[name + "_2"] = value
    return out


def reference(
    x, w_in, b_gate, norm_mix, norm_ffn, hgrn_lb_logits, hgrn_out_gain, q_gain, k_gain,
    rel_bias, w_proj_a, w_proj_b, w_out, w_ffn_in, w_ffn_out, c_2, w_ada_2, b_ada_2,
    pre_norm_mix_2, post_norm_mix_2, w_in_2, cmp_k_pos_2, cmp_k_w1_2, cmp_k_w2_2, cmp_v_pos_2,
    cmp_v_w1_2, cmp_v_w2_2, w_o_2, pre_norm_ffn_2, post_norm_ffn_2, w_up_2, w_down_2,
):
    x = first_block(
        x, w_in, b_gate, norm_mix, norm_ffn, hgrn_lb_logits, hgrn_out_gain, q_gain, k_gain,
        rel_bias, w_proj_a, w_proj_b, w_out, w_ffn_in, w_ffn_out,
    )
    return second_block(
        x, c_2, w_ada_2, b_ada_2, pre_norm_mix_2, post_norm_mix_2, w_in_2, cmp_k_pos_2,
        cmp_k_w1_2, cmp_k_w2_2, cmp_v_pos_2, cmp_v_w1_2, cmp_v_w2_2, w_o_2, pre_norm_ffn_2,
        post_norm_ffn_2, w_up_2, w_down_2,
    )


_drawn_inputs = setup_inputs


def setup_inputs(seed=0):
    import zlib

    import numpy as np

    out = dict(_drawn_inputs(seed))
    spreads = {}
    factors = {'b_gate': 8.0,
     'norm_mix': 5.456,
     'norm_ffn': 15.317,
     'hgrn_lb_logits': 2.867,
     'hgrn_out_gain': 7.875,
     'q_gain': 8.0,
     'k_gain': 8.0,
     'rel_bias': 22.733,
     'b_ada_2': 12.529,
     'pre_norm_mix_2': 47.143,
     'post_norm_mix_2': 200.0,
     'cmp_k_pos_2': 64.0,
     'cmp_v_pos_2': 165.602,
     'pre_norm_ffn_2': 200.0,
     'post_norm_ffn_2': 200.0,
     'cmp_k_w1_2': 4.017,
     'cmp_k_w2_2': 4.114,
     'cmp_v_w1_2': 3.511,
     'cmp_v_w2_2': 2.873}
    for name, (base, spread) in spreads.items():
        noise = np.random.default_rng([zlib.crc32(name.encode()), seed]).standard_normal(out[name].shape)
        drawn = base * np.exp(spread * noise) if base else spread * noise
        out[name] = __import__('jax').numpy.asarray(drawn.astype(out[name].dtype))
    for name, factor in factors.items():
        out[name] = (out[name] * factor).astype(out[name].dtype)
    return out
```

```python
from contextlib import ExitStack

import numpy as np

import concourse.bass as bass
from concourse import mybir

F32 = mybir.dt.float32
F32R = mybir.dt.float32r
U8 = mybir.dt.uint8
ACT = mybir.ActivationFunctionType
ALU = mybir.AluOpType
AX = mybir.AxisListType
ds = bass.ds

P = 128
T = 256
TT = T // P
D = 2048
KT = D // P
H = 8
DA = H * P
N_GATE = 24
CHUNK = 64
N_REL = 191
REL_FUTURE = CHUNK - 1
D_FF1 = 5632
D_FF2 = 8192
CMP_LEN, CMP_STRIDE = 32, 16
N_CMP = (T - CMP_LEN) // CMP_STRIDE + 1
EPS = 1e-6
SCALE = float(P) ** -0.5
MASKED = -1e30
MAX_FLOOR = -1e29
TINY = 1e-30

KU = 2
GCOL = 512
UW = KU * GCOL
NRAW = 4
NSPLIT = 4
GT = GCOL // P
BLK = H * T

COLS = {}
_at = 0
for _name, _n in (("norm_mix", 16), ("norm_ffn", 16), ("b_gate", 32), ("lb", 16), ("out_gain", 8), ("q_gain", 1),
                  ("k_gain", 1), ("c", 16), ("b_ada", 96), ("pre_mix", 16), ("post_mix", 16), ("pre_ffn", 16),
                  ("post_ffn", 16), ("k_pos", 32), ("v_pos", 32)):
    COLS[_name] = _at
    _at += _n
N_COLS = _at

CONST = {}
_at = 0
for _name, _n in (("ident", 128), ("flip", 128), ("swap", 128), ("ones", 128), ("cos", 256), ("sin", 256),
                  ("causal", 256), ("chunk", 256), ("cmp", 256), ("eps", 1)):
    CONST[_name] = _at
    _at += _n
N_CONST = _at
N_LEVEL = 8
EXT = 384


def constants():
    c = np.zeros((P, N_CONST), np.float32)
    i = np.arange(P)
    put = lambda name, a: c.__setitem__((slice(None), slice(CONST[name], CONST[name] + a.shape[1])), a)
    put("ident", np.eye(P, dtype=np.float32))
    put("flip", np.eye(P, dtype=np.float32)[::-1])
    put("swap", np.roll(np.eye(P, dtype=np.float32), P // 2, axis=0))
    put("ones", np.ones((P, P), np.float32))
    inv = np.float32(10000.0) ** (-np.arange(0, P, 2, dtype=np.float32) / np.float32(P))
    ang = (np.arange(T, dtype=np.float32)[:, None] * inv[None, :]).astype(np.float32).T
    put("cos", np.concatenate([np.cos(ang), np.cos(ang)]).astype(np.float32))
    put("sin", np.concatenate([-np.sin(ang), np.sin(ang)]).astype(np.float32))
    tri = np.where(i[None, :] > i[:, None], np.float32(MASKED), np.float32(0))
    put("causal", np.concatenate([np.zeros((P, P), np.float32), tri], 1))
    ch = np.where(i[None, :] // CHUNK > i[:, None] // CHUNK, np.float32(MASKED), np.float32(0))
    put("chunk", np.concatenate([np.zeros((P, P), np.float32), ch], 1))
    end = i * CMP_STRIDE + CMP_LEN - 1
    cm = [np.where((i[None, :] < N_CMP) & (end[None, :] <= t0 + i[:, None]), np.float32(0), np.float32(MASKED))
          for t0 in (0, P)]
    put("cmp", np.concatenate(cm, 1))
    put("eps", np.full((P, 1), EPS, np.float32))
    m = np.zeros((P, N_LEVEL, P), np.float32)
    m[:, 0] = np.eye(P, dtype=np.float32)
    s, t = i[:, None], i[None, :]
    for lev in range(1, N_LEVEL):
        b = 1 << (lev - 1)
        m[:, lev] = (s // (2 * b) == t // (2 * b)) & (s % (2 * b) < b) & (t % (2 * b) >= b)
    return c, m.reshape(P, N_LEVEL * P)


PHASES = {}


def plan():
    u = v = g = 0
    for name, groups, units, ada in (
            ("f", 2, 8, 0), ("q", 2, 8, 0), ("i", 2, 8, 0), ("g", 2, 8, 0), ("qb", 2, 8, 0), ("kb", 2, 8, 0),
            ("vb", 2, 8, 0), ("gate_a", 4, 8, 0), ("proj_a", 4, 4, 0), ("gate_b", 4, 8, 0), ("proj_b", 4, 4, 0),
            ("out", 4, 8, 4), ("ffn1", 66, 4, 0), ("cmp_kv", 1, 8, 0), ("qn", 2, 8, 0), ("cmp", 2, 4, 0),
            ("selwin", 2, 8, 0), ("moba", 6, 8, 0), ("wo", 8, 4, 0), ("ffn2", 48, 4, 0)):
        PHASES[name] = (u, v, g)
        if name == "ffn1":
            u, v, g = u + 11 * 40, v + 11 * 24, g + 11 * 6
            continue
        u += groups * (units + ada)
        v += groups * units
        g += 0 if name == "cmp" else groups


plan()


class Place:

    def __init__(self):
        self.u = self.v = self.g = self.a = 0
        self.ou = self.ov = self.og = self.oa = 0

    def enter(self, i, u, v, g, a=0):
        self.ou, self.ov, self.og, self.oa = i * u, i * v, i * g, i * a

    def leave(self, n, u, v, g, a=0):
        self.ou = self.ov = self.og = self.oa = 0
        self.u += (n - 1) * u
        self.v += (n - 1) * v
        self.g += (n - 1) * g
        self.a += (n - 1) * a


def build(nc, A, out, scratch):
    with ExitStack() as ctx:
        def sb(name, shape, dt=F32):
            return ctx.enter_context(nc.sbuf_tensor(name, shape, dt))

        sems = {}

        def S(name):
            if name not in sems:
                sems[name] = ctx.enter_context(nc.semaphore(name))
            return sems[name]

        raw = sb("raw", [P, NRAW, UW])
        whi = sb("whi", [P, NSPLIT, UW], F32R)
        wlo = sb("wlo", [P, NSPLIT, UW], F32R)
        hH = sb("hH", [P, KT, T], F32R)
        hL = sb("hL", [P, KT, T], F32R)
        yH = sb("yH", [P, H, T], F32R)
        yL = sb("yL", [P, H, T], F32R)
        arena = sb("arena", [P, 11 * BLK + BLK // 2])
        cst = sb("cst", [P, N_CONST])
        col = sb("col", [P, N_COLS])
        lmask = sb("lmask", [P, N_LEVEL * P], U8)
        rstd = sb("rstd", [P, T])
        red = sb("red", [P, T])
        small = sb("small", [P, 64])
        lb = sb("lb", [P, 6, H])
        rr = sb("rr", [P, 2, 2 * H])
        cs = sb("cs", [P, KT])
        mod = sb("mod", [P, 96])
        modA = sb("modA", [P, 4, KT])
        stat = sb("stat", [P, 4, 3, 2])
        gates = sb("gates", [P, TT, N_GATE])
        wgh = sb("wgh", [P, KT, N_GATE], F32R)
        wgl = sb("wgl", [P, KT, N_GATE], F32R)

        acc = ctx.enter_context(nc.psum_tensor("acc", [P, 2, 2 * GCOL], F32))
        W = ctx.enter_context(nc.psum_tensor("W", [P, 4, 512], F32))
        Wf = W[:].rearrange("p a b -> p (a b)")

        def blk(i, n=1):
            return arena[:, i * BLK:int((i + n) * BLK)]

        def tiles(ap, t=T):
            return ap.rearrange("p (k t) -> p k t", t=t)

        def C(name, n=P):
            return cst[:, CONST[name]:CONST[name] + n]

        def V(name, n=1, at=0):
            return col[:, COLS[name] + at:COLS[name] + at + n]

        ident, ones, flip, swap = C("ident"), C("ones"), C("flip"), C("swap")
        one = C("ones", 1)
        epsc = C("eps", 1)
        x0 = tiles(blk(0, 2))
        sq0 = tiles(blk(2, 2))
        qa, ka, ia, ga = blk(0), blk(1), blk(2), blk(3)
        qb, kb, vb = blk(4), blk(5), blk(6)
        bc, Cb, ST, ob = blk(7), blk(8), blk(9), blk(10)
        off = blk(11, 0.5)
        iav = ia.rearrange("p (t n) -> p t n", t=TT)
        vbv = vb.rearrange("p (t n) -> p t n", t=TT)
        lmaskf = blk(4, 0.5)
        M = blk(0, 2)
        HK = blk(3)
        yb = blk(7)
        sgb = blk(8, 2)
        sb3 = blk(10)[:, 0:3 * 384].rearrange("p (r n) -> p r n", r=3)
        pt2 = blk(11, 0.5)[:, 0:2 * 384].rearrange("p (r n) -> p r n", r=2)
        X = tiles(blk(2, 2))
        gtmp = blk(4, 0.5)
        act32 = blk(5)
        O32 = tiles(blk(0, 2))
        kvc = tiles(blk(0, 0.5))
        ksel, kwin = tiles(arena[:, 1024:1536]), tiles(arena[:, 1536:2048])
        vsel = arena[:, 2048:2560].rearrange("p (t n) -> p t n", t=TT)
        vwin = arena[:, 2560:3072].rearrange("p (t n) -> p t n", t=TT)
        cx = blk(9)
        hidP = W[:, 3, 0:64].rearrange("p (k c) -> p k c", k=2)
        hid = arena[:, 3072:3584].rearrange("p (k g c) -> p k g c", k=2, g=2)
        kcT = arena[:, 3584:3840].rearrange("p (g c) -> p g c", g=2)
        vcm = arena[:, 3840:4096].rearrange("p (g d) -> p g d", g=2)
        qn, qm, km, vm, on, om = blk(4), blk(5), blk(6), blk(7), blk(8), blk(9)
        vmv = vm.rearrange("p (t n) -> p t n", t=TT)
        hsg = sb("hsg", [P, 2, 32])
        rope = blk(10)[:, 3 * 384:3 * 384 + GCOL]
        adaacc = blk(6).rearrange("p (r e n) -> p r e n", r=2, e=2)
        wg = blk(7)[:, 0:KT * N_GATE].rearrange("p (k n) -> p k n", k=KT)
        w2 = blk(7)[:, 384:384 + 2 * P].rearrange("p (k n) -> p k n", k=2)
        ext = arena[0:H, 10 * BLK:10 * BLK + EXT]
        modP = W[:, 2, 0:96]

        wv = {n: A[n].rearrange("(k p) n -> p k n", p=P) for n in
              ("w_in", "w_proj_a", "w_proj_b", "w_out", "w_ffn_in", "w_ffn_out", "w_ada_2", "w_in_2", "w_o_2",
               "w_up_2", "w_down_2", "cmp_k_w1_2", "cmp_v_w1_2")}
        landed = [S(f"landed{i}") for i in range(NRAW)]

        jobs = []
        for h in range(H):
            hd = slice(h * T, (h + 1) * T)
            jobs.append(("bias", qb[:, hd], kb[:, hd], [vbv[:, t, h * P:(h + 1) * P] for t in range(TT)],
                         yb[:, hd], h, True, True, None))
        N_B = len(jobs)
        for h in range(H):
            hd, g = slice(h * T, (h + 1) * T), h // 4
            gt = [gates[:, t, 3 * h:3 * h + 3] for t in range(TT)]
            jobs.append(("causal", qn[:, hd], ksel[:, g], [vsel[:, t, g * P:(g + 1) * P] for t in range(TT)],
                         on[:, hd], H + h, True, False, [x[:, 1:2] for x in gt]))
            jobs.append(("causal", qn[:, hd], kwin[:, g], [vwin[:, t, g * P:(g + 1) * P] for t in range(TT)],
                         on[:, hd], H + h, False, False, [x[:, 2:3] for x in gt]))
            jobs.append(("cmp", qn[:, hd], kcT[:, g], [vcm[:, g]], on[:, hd], H + h, False, True,
                         [x[:, 0:1] for x in gt]))
        N_N = len(jobs)
        for h in range(H):
            hd = slice(h * T, (h + 1) * T)
            jobs.append(("causal", qm[:, hd], km[:, hd], [vmv[:, t, h * P:(h + 1) * P] for t in range(TT)],
                         om[:, hd], 2 * H + h, True, True, None))
        N_M = len(jobs)
        last_of = {j[5]: n for n, j in enumerate(jobs) if j[7]}

        def parts(kind):
            return [(0, P), (P, 2 * P if kind == "cmp" else 3 * P)]

        def mask_of(kind, t):
            if kind == "cmp":
                return cst[:, CONST["cmp"] + t * P:CONST["cmp"] + (t + 1) * P]
            at = CONST["chunk" if kind == "bias" else "causal"]
            return cst[:, at + P:at + 2 * P] if t == 0 else cst[:, at:at + 2 * P]

        block = ctx.enter_context(nc.Block())

        @block.sync
        def _(sp):
            pl = Place()

            def load(src, shape=None):
                s = pl.u % NRAW
                if pl.u >= NRAW:
                    sp.wait_ge(S("unit_done"), pl.u + pl.ou - NRAW + 1)
                dst = raw[:, s].rearrange("p (k n) -> p k n", k=shape or KU)
                sp.dma_start(dst, src).then_inc(landed[s], 16)
                pl.u += 1

            def group(w, c0, units, k0=0):
                for u in range(units):
                    load(wv[w][:, k0 + u * KU:k0 + (u + 1) * KU, c0:c0 + GCOL])

            def looped(w, c0, groups, units, k0=0):
                with sp.Fori(0, groups) as i:
                    pl.enter(i, units, 0, 0)
                    for u in range(units):
                        load(wv[w][:, k0 + u * KU:k0 + (u + 1) * KU, ds(i * GCOL + c0, GCOL)])
                pl.leave(groups, units, 0, 0)

            sp.dma_start(x0, A["xT"].rearrange("(k p) t -> p k t", p=P)).then_inc(S("x_in"), 16)
            sp.dma_start(col[:], A["cols"]).then_inc(S("x_in"), 16)
            sp.dma_start(cst[:], A["consts"]).then_inc(S("x_in"), 16)
            sp.dma_start(lmaskf, A["lmask"]).then_inc(S("x_in"), 16)
            group("w_in", DA, 8)
            group("w_in", DA + GCOL, 8)
            looped("w_in", 0, 2, 8)
            looped("w_in", 2 * DA, 2, 8)
            looped("w_in", 3 * DA, 12, 8)
            looped("w_proj_a", 0, 4, 4)
            looped("w_in", 7 * DA + D, 4, 8)
            looped("w_proj_b", 0, 4, 4)
            with sp.Fori(0, 2) as i:
                pl.enter(i, 24, 0, 0)
                for j in range(2):
                    for u in range(4):
                        k0 = (4 * j + u) * KU
                        load(wv["w_ada_2"][:, k0:k0 + KU, ds(i * GCOL, GCOL)])
                    for u in range(8):
                        load(wv["w_out"][:, u * KU:(u + 1) * KU, ds(i * 2 * GCOL + j * GCOL, GCOL)])
            pl.leave(2, 24, 0, 0)

            def ffn1(i, down):
                for half in range(2):
                    for u in range(8):
                        load(wv["w_ffn_in"][:, u * KU:(u + 1) * KU, ds(i * GCOL + half * D_FF1, GCOL)])
                    for u in range(8):
                        load(wv["w_ada_2"][:, u * KU:(u + 1) * KU, ds(i * 2 * GCOL + (2 + half) * GCOL, GCOL)])
                if down:
                    for g in range(4):
                        for u in range(2):
                            load(wv["w_ffn_out"][:, ds(i * GT + (u * KU - GT), KU), g * GCOL:(g + 1) * GCOL])

            ffn1(0, False)
            with sp.Fori(0, 10) as i:
                pl.enter(i, 40, 0, 0)
                ffn1(i + 1, True)
            pl.leave(10, 40, 0, 0)
            for g in range(4):
                group_k = D_FF1 // P - GT
                for u in range(2):
                    load(wv["w_ffn_out"][:, group_k + u * KU:group_k + (u + 1) * KU, g * GCOL:(g + 1) * GCOL])

            group("w_in_2", DA, 8)
            looped("w_in_2", 0, 2, 8)
            for w in ("cmp_k_w1_2", "cmp_v_w1_2"):
                for u in range(4):
                    load(wv[w][:, u * 8:(u + 1) * 8, :], shape=8)
            looped("w_in_2", DA + GCOL, 2, 8)
            looped("w_in_2", DA + 3 * GCOL + N_GATE, 6, 8)
            looped("w_o_2", 0, 4, 4)
            looped("w_o_2", 0, 4, 4, k0=8)

            def up(i):
                for j in range(2):
                    for u in range(8):
                        load(wv["w_up_2"][:, u * KU:(u + 1) * KU, ds(i * 2 * GCOL + j * GCOL, GCOL)])

            def down(i):
                for g in range(4):
                    for u in range(4):
                        load(wv["w_down_2"][:, ds(i * 8 + u * KU, KU), g * GCOL:(g + 1) * GCOL])

            up(0)
            with sp.Fori(0, 7) as i:
                pl.enter(i, 32, 0, 0)
                up(i + 1)
                down(i)
            pl.leave(7, 32, 0, 0)
            down(7)
            sp.wait_ge(S("x_done"), 1)
            sp.dma_start(out.rearrange("(k p) t -> p k t", p=P), X).then_inc(S("stored"), 16)
            sp.wait_ge(S("stored"), 16)

        @block.gpsimd
        def _(pool):
            pool.memset(ST, 0.0).then_inc(S("st_zero"), 1)
            pool.dma_start(ext[:, P:P + N_REL], A["rel_rev"]).then_inc(S("ext_in"), 16)
            pool.wait_ge(S("ext_full"), 2)
            pool.dma_start(scratch, ext).then_inc(S("ext_out"), 16)
            pool.wait_ge(S("ext_out"), 16)
            pool.wait_ge(S("hn_done"), 1)
            src = bass.AP(scratch.tensor, 0, [[1, P], [EXT, H], [1, T]])
            pool.dma_start(tiles(HK), src).then_inc(S("hk_in"), 16)
            pool.wait_ge(S("att_s"), N_B)
            pool.dma_start(X, A["xT"].rearrange("(k p) t -> p k t", p=P)).then_inc(S("x_again"), 16)
            pool.wait_ge(S("merged"), 4)
            pool.dma_start(wg, wv["w_in_2"][:, :, DA + 3 * GCOL:DA + 3 * GCOL + N_GATE]).then_inc(S("wg_in"), 16)
            pool.dma_start(w2[:, 0], A["cmp_k_w2_2"]).then_inc(S("wg_in"), 16)
            pool.dma_start(w2[:, 1], A["cmp_v_w2_2"]).then_inc(S("wg_in"), 16)
            pool.wait_ge(S("h_lo"), 12)
            pool.memset(hid.rearrange("p k g c -> p (k g c)"), 0.0).then_inc(S("hid_zero"), 1)
            pool.wait_ge(S("h_lo"), 16)
            pool.memset(blk(0, 2), 0.0).then_inc(S("o_zero"), 1)

        @block.scalar
        def _(act):
            pl = Place()

            def hi():
                s, v = pl.u % NRAW, pl.v % NSPLIT
                act.wait_ge(landed[s], 16 * (pl.u // NRAW + 1) + pl.ou * (16 // NRAW))
                if pl.v >= NSPLIT:
                    act.wait_ge(S("w_used"), pl.v + pl.ov - NSPLIT + 1)
                act.activation(whi[:, v], raw[:, s], ACT.Copy).then_inc(S("w_hi"), 1)
                pl.u += 1
                pl.v += 1

            def group(units=8, hooks={}, begin=0):
                for u in range(begin, units):
                    hi()
                    if u in hooks:
                        hooks[u]()
                pl.g += 1

            def full(g, v):
                act.wait_ge(S("w_used"), v)
                return acc[:, g % 2]

            def norm_stats(k, src, sq):
                act.activation(sq, src, ACT.Square).then_inc(S("nm_sq"), 1)
                act.wait_ge(S("nm_sum"), k + 1)
                act.activation(rstd[:], W[:, 3, 0:T], ACT.Sqrt, bias=epsc, scale=1.0 / D).then_inc(S("nm_root"), 1)

            def norm_hi(k, h32):
                for c in range(4):
                    act.wait_ge(S("h_ready"), 4 * k + c + 1)
                    act.activation(hH[:, 4 * c:4 * c + 4], h32[:, 4 * c:4 * c + 4], ACT.Copy).then_inc(S("h_hi"), 1)

            act.wait_ge(S("x_in"), 64)
            act.wait_ge(S("lb_step"), 1)
            act.activation(lb[:, 0:2], lb[:, 0:2], ACT.Exp).then_inc(S("lb_exp"), 1)
            act.activation(cs[:], V("c", 16), ACT.Sigmoid).then_inc(S("c_sig"), 1)
            for _ in range(4):
                hi()
            norm_stats(0, x0, sq0)
            norm_hi(0, sq0)

            def evac_sig(g, v, dst, sem):
                def run():
                    a = full(g, v)
                    ins = act.activation(dst, a, ACT.Sigmoid)
                    ins.then_inc(S(sem), 1)
                return run

            def evac_copy(g, v, dst, sem, tokens=False):
                def run():
                    a = full(g, v)
                    if tokens:
                        a = a.rearrange("p (t n) -> p t n", t=TT)
                    act.activation(dst, a, ACT.Copy).then_inc(S(sem), 1)
                return run

            def half(b, i):
                return b[:, i * 1024:(i + 1) * 1024]

            def halfv(b, i):
                return b[:, :, i * GCOL:(i + 1) * GCOL]

            def level_exp(l):
                def run():
                    act.wait_ge(S("c_diff"), l)
                    if l < 8:
                        b = 1 << (l - 1)
                        v = Cb.rearrange("p (n h b) -> p n h b", h=2, b=b)
                        act.activation(v[:, :, 0], v[:, :, 0], ACT.Exp, scale=-1.0)
                        act.activation(v[:, :, 1], v[:, :, 1], ACT.Exp).then_inc(S("c_exp"), 1)
                    else:
                        v = Cb.rearrange("p (h t s) -> p h t s", h=H, t=TT)
                        bv = bc.rearrange("p (h t s) -> p h t s", h=H, t=TT)
                        act.activation(v[:, :, 0], v[:, :, 0], ACT.Exp, scale=-1.0)
                        act.activation(v[:, :, 1], bv[:, :, 1], ACT.Exp).then_inc(S("c_exp"), 1)
                return run

            group(begin=4)
            group(hooks={3: evac_sig(0, 8, half(ka, 0), "sig_f")})
            group(hooks={3: evac_sig(1, 16, half(ka, 1), "sig_f")})
            def sig_q(g, v, i):
                return evac_sig(g, v, half(qa, i), "sig_q")
            group(hooks={3: sig_q(2, 24, 0)})

            def ln_f():
                act.wait_ge(S("f_in"), 2)
                act.activation(Cb, Cb, ACT.Ln).then_inc(S("ln_f"), 1)
            group(hooks={3: sig_q(3, 32, 1), 5: ln_f})
            group(hooks={3: evac_copy(4, 40, halfv(iav, 0), "i_in", True)})
            group(hooks={3: evac_copy(5, 48, halfv(iav, 1), "i_in", True)})
            group(hooks={3: evac_sig(6, 56, half(ga, 0), "sig_g"), 6: level_exp(1)})
            group(hooks={3: evac_sig(7, 64, half(ga, 1), "sig_g"), 6: level_exp(2)})
            group(hooks={3: evac_copy(8, 72, half(qb, 0), "qk_in"), 6: level_exp(3)})
            group(hooks={3: evac_copy(9, 80, half(qb, 1), "qk_in"), 6: level_exp(4)})
            group(hooks={3: evac_copy(10, 88, half(kb, 0), "qk_in"), 6: level_exp(5)})
            group(hooks={3: evac_copy(11, 96, half(kb, 1), "qk_in"), 6: level_exp(6)})
            group(hooks={3: evac_copy(12, 104, halfv(vbv, 0), "vb_in", True), 6: level_exp(7)})

            def off_copy():
                act.wait_ge(S("lvl"), 9)
                act.activation(off, Wf[:, 0:H * P], ACT.Copy).then_inc(S("off_in"), 1)

            def head_square(k):
                def run():
                    src = (ob, qb, kb)[k]
                    if k == 0:
                        act.wait_ge(S("o_mm"), 1)
                        act.wait_ge(S("ext_out"), 16)
                        act.activation(ob, Wf, ACT.Copy).then_inc(S("o_in"), 1)
                        act.wait_ge(S("o_in"), 1)
                    else:
                        act.wait_ge(S("hn_sum"), k)
                        act.wait_ge(S("qk_in"), 4)
                    act.activation(Cb, src, ACT.Square).then_inc(S("hn_sq"), 1)
                return run

            def head_root(k):
                def run():
                    act.wait_ge(S("hn_sum"), k + 1)
                    act.activation(rr[:, 0], W[:, 3, 0:2 * H], ACT.Sqrt, bias=epsc, scale=1.0 / P)\
                       .then_inc(S("hn_root"), 1)
                return run

            def ya_hi():
                act.wait_ge(S("hn_done"), 1)
                act.activation(yH[:], tiles(ob), ACT.Copy).then_inc(S("y_hi"), 1)

            def gate_sig(g, v, dst, at):
                def run():
                    a = full(g, v)
                    for m in range(GT):
                        ins = act.activation(dst[:, m * T:(m + 1) * T], a[:, m * T:(m + 1) * T], ACT.Sigmoid,
                                             bias=V("b_gate", 1, at + m))
                    ins.then_inc(S("gate_in"), 1)
                return run

            group(hooks={3: evac_copy(13, 112, halfv(vbv, 1), "vb_in", True), 6: level_exp(8)})

            def mg(i):
                return M[:, i * 1024:(i + 1) * 1024]

            def first_gate():
                act.wait_ge(S("c_done"), 8)
                gate_sig(14, 120, mg(0), 0)()
            group(hooks={2: off_copy, 3: first_gate, 5: head_square(0)})
            group(hooks={0: head_root(0), 1: head_square(1), 3: gate_sig(15, 128, mg(1), 4),
                         4: ya_hi, 5: head_root(1), 6: head_square(2)})
            group(hooks={2: head_root(2), 3: gate_sig(16, 136, mg(2), 8)})

            def att(n, n0, n1):
                if n0 <= n - 3 < n1 and jobs[n - 3][7]:
                    kind, q, k, vs, y, head, fst, lst, gt = jobs[n - 3]
                    act.wait_ge(S("att_pv"), n - 3 + 1)
                    act.activation(y, W[:, 3, (head % 2) * T:(head % 2 + 1) * T], ACT.Copy)\
                       .then_inc(S("att_y"), 1)
                if n0 <= n - 2 < n1:
                    m = n - 2
                    width = parts(jobs[m][0])[1][1]
                    act.wait_ge(S("att_t"), m + 1)
                    if m >= 2:
                        act.wait_ge(S("att_pv"), m - 1)
                    act.activation(pt2[:, m % 2, 0:width], W[:, 2, 0:width], ACT.Copy).then_inc(S("att_pt"), 1)
                if n0 <= n < n1:
                    kind = jobs[n][0]
                    act.wait_ge(S("att_neg"), n + 1)
                    for t, (a, b) in enumerate(parts(kind)):
                        p = sb3[:, n % 3, a:b]
                        ins = act.activation(p, p, ACT.Exp, bias=stat[:, 1, n % 3, t:t + 1],
                                             scale=1.0 if kind == "bias" else SCALE,
                                             accum_out=stat[:, 2, n % 3, t:t + 1])
                    ins.then_inc(S("att_exp"), 1)

            def slot(n, n0, n1):
                return lambda: att(n, n0, n1)

            g0, v0 = PHASES["proj_a"][2], PHASES["proj_a"][1]
            group(4, hooks={2: slot(0, 0, N_B), 3: gate_sig(17, 144, mg(3), 12)})
            for i in range(1, 4):
                group(4, hooks={2: slot(i, 0, N_B)})
            sg = lambda i: sgb[:, i * 1024:(i + 1) * 1024]
            for i in range(4):
                hooks = {2: slot(4 + 2 * i, 0, N_B), 6: slot(5 + 2 * i, 0, N_B)}
                if i:
                    hooks[3] = gate_sig(22 + i - 1, PHASES["gate_b"][1] + 8 * i, sg(i - 1), 16 + 4 * (i - 1))
                group(hooks=hooks)

            def yb_hi():
                act.wait_ge(S("w_used"), PHASES["gate_b"][1])
                act.wait_ge(S("att_y"), H)
                act.activation(yH[:], tiles(yb), ACT.Copy).then_inc(S("y_hi"), 1)
            for _ in range(4):
                hi()
            gate_sig(25, PHASES["gate_b"][1] + 32, sg(3), 28)()
            yb_hi()
            pl.g += 1
            for i in range(1, 4):
                group(4)
            def ada4():
                pl.u += 4

            ada4()
            for _ in range(4):
                hi()
            for c in range(4):
                act.wait_ge(S("merged"), c + 1)
                act.activation(hH[:, 4 * c:4 * c + 4], tiles(M)[:, 4 * c:4 * c + 4], ACT.Copy).then_inc(S("m_hi"), 1)
            for _ in range(4):
                hi()
            pl.g += 1
            for i in range(1, 4):
                ada4()
                group()
            for _ in range(4):
                hi()
            act.wait_ge(S("x1"), 4)
            norm_stats(1, X, tiles(M))
            norm_hi(1, tiles(M))

            G1 = PHASES["ffn1"][2]

            def ffn_sig(g, vpos):
                act.wait_ge(S("w_used"), vpos)
                act.activation(gtmp, acc[:, g % 2], ACT.Sigmoid).then_inc(S("ff_sig"), 1)

            def ffn1(begin, down, n):
                if down:
                    hi(); hi(); hi(); hi()
                    act.wait_ge(S("ff_act"), n)
                    act.wait_ge(S("w_used"), pl.v + pl.ov - 4)
                    act.activation(yH[:, 0:GT], tiles(act32[:, 0:1024]), ACT.Copy).then_inc(S("ff_hi"), 1)
                    hi(); hi(); hi(); hi()
                else:
                    for _ in range(begin, 8):
                        hi()
                pl.u += 8
                for _ in range(4):
                    hi()
                ffn_sig(pl.g, pl.v + pl.ov - 4)
                for _ in range(4):
                    hi()
                pl.u += 8
                if down:
                    for _ in range(8):
                        hi()
                pl.g += 6 if down else 2

            ffn1(4, False, 0)
            with act.Fori(0, 10) as i:
                pl.enter(i, 40, 24, 6)
                ffn1(0, True, i + 1)
            pl.leave(10, 40, 24, 6)
            for _ in range(4):
                hi()
            act.wait_ge(S("ff_act"), 11)
            act.wait_ge(S("w_used"), pl.v - 4)
            act.activation(yH[:, 0:GT], tiles(act32[:, 0:1024]), ACT.Copy).then_inc(S("ff_hi"), 1)
            for _ in range(4):
                hi()
            pl.g += 4
            for _ in range(4):
                hi()
            act.wait_ge(S("ff_sum"), 44)
            norm_stats(2, X, O32)
            norm_hi(2, O32)
            act.wait_ge(S("wg_in"), 48)
            act.activation(wgh[:], wg[:], ACT.Copy).then_inc(S("wg_hi"), 1)

            def rope_raw(n, g, v, c0, width, vdst=None):
                def run():
                    act.wait_ge(S("w_used"), v)
                    if vdst is not None:
                        act.activation(vdst, acc[:, g % 2, GCOL:].rearrange("p (t n) -> p t n", t=TT), ACT.Copy)\
                           .then_inc(S("kv_in"), 1)
                    if n >= 1:
                        act.wait_ge(S("roped"), n)
                    act.activation(rope[:, 0:width], acc[:, g % 2, c0:c0 + width], ACT.Copy).then_inc(S("rope_raw"), 1)
                return run

            v2, gg = PHASES["cmp_kv"][1], PHASES["cmp_kv"][2]
            group(begin=4)
            group(hooks={3: rope_raw(0, gg, v2 + 8, 0, GCOL, kvc[:, 2:4])})

            def x_hi(kind):
                def run():
                    act.wait_ge(S("cx"), kind + 1)
                    act.activation(yH[:].rearrange("p a b -> p (a b)")[:, kind * 1024:kind * 1024 + 960],
                                   cx[:, kind * 1024:kind * 1024 + 960], ACT.Copy).then_inc(S("cx_hi"), 1)
                return run
            group(hooks={3: rope_raw(1, gg + 1, v2 + 16, 0, GCOL), 4: x_hi(0), 5: x_hi(1),
                         7: rope_raw(2, gg + 1, v2 + 16, GCOL, GCOL)})
            for _ in range(4):
                hi()
            rope_raw(3, gg + 2, v2 + 24, 0, GCOL)()
            for _ in range(4):
                hi()
            rope_raw(4, gg + 2, v2 + 24, GCOL, GCOL)()

            def hid_sig():
                act.wait_ge(S("w_used"), v2 + 32)
                act.activation(hsg[:, :, 0:30], hidP[:, :, 0:30], ACT.Sigmoid).then_inc(S("hid_sig"), 1)

            def gates_sig():
                act.wait_ge(S("gates_mm"), 1)
                act.activation(gates[:].rearrange("p t n -> p (t n)"), W[:, 2, 0:TT * N_GATE], ACT.Sigmoid)\
                   .then_inc(S("gates_in"), 1)

            def kvc_copy():
                act.wait_ge(S("cmp_kv"), 1)
                act.activation(kcT.rearrange("p g c -> p (g c)"), W[:, 0, 0:2 * P], ACT.Copy)
                act.activation(vcm.rearrange("p g c -> p (g c)"), W[:, 0, 2 * P:4 * P], ACT.Copy)\
                   .then_inc(S("kvc_in"), 1)
            group(hooks={4: hid_sig, 6: gates_sig})
            group(hooks={3: rope_raw(5, gg + 3, v2 + 40, 0, GCOL, vsel), 4: kvc_copy})

            def also(*fs):
                return lambda: [f() for f in fs]
            n = N_B
            for j in range(6):
                hooks = {}
                for u in ((3, 6, 7) if j == 0 else (1, 3, 5, 7)):
                    hooks[u] = slot(n, N_B, N_N)
                    n += 1
                end = v2 + 48 + 8 * j
                if j == 0:
                    hooks[3] = also(rope_raw(6, gg + 4, end, 0, GCOL, vwin), hooks[3])
                elif j <= 4:
                    r = 7 + 2 * (j - 1)
                    hooks[3] = also(hooks[3], rope_raw(r, gg + 4 + j, end, 0, GCOL))
                    hooks[7] = also(hooks[7], rope_raw(r + 1, gg + 4 + j, end, GCOL, GCOL))
                else:
                    hooks[3] = also(hooks[3], evac_copy(gg + 9, end, halfv(vmv, 0), "vm_in", True))
                group(hooks=hooks)
            for u in range(3):
                hi()
                att(n, N_B, N_N)
                n += 1
            hi()
            evac_copy(gg + 10, v2 + 96, halfv(vmv, 1), "vm_in", True)()
            att(n, N_B, N_N)
            assert n == N_N + 2
            act.wait_ge(S("att_y"), 2 * H)
            act.activation(yH[:], tiles(on), ACT.Copy).then_inc(S("y_hi"), 1)
            pl.g += 1
            n = N_N
            gw, vw = PHASES["wo"][2], PHASES["wo"][1]

            def wo_copy(i):
                return evac_copy(gw + i, vw + 4 * (i + 1), blk(0, 2)[:, i * 1024:(i + 1) * 1024], "wo_in")
            for i in range(1, 4):
                group(4, hooks={1: slot(n, N_N, N_M), 2: slot(n + 1, N_N, N_M),
                                3: also(wo_copy(i - 1), slot(n + 2, N_N, N_M))})
                n += 3
            hi()
            hi()
            att(n, N_N, N_M)
            hi()
            hi()
            wo_copy(3)()
            att(n + 1, N_N, N_M)
            assert n + 1 == N_M + 2
            act.wait_ge(S("att_y"), 3 * H)
            act.activation(hH[:, 0:8], tiles(om), ACT.Copy).then_inc(S("om_hi"), 1)
            pl.g += 1
            for i in range(1, 4):
                group(4)
            for _ in range(4):
                hi()
            act.wait_ge(S("o_sum"), 4)
            norm_stats(3, O32, tiles(blk(4, 2)))
            act.wait_ge(S("x_mix"), 1)
            norm_stats(4, X, O32)
            norm_hi(3, O32)

            def up(begin, n, prev):
                for u in range(begin, 4):
                    hi()
                if prev:
                    act.wait_ge(S("w_used"), pl.v + pl.ov - 4)
                    act.wait_ge(S("f2_act"), 2 * n)
                    act.activation(yH[:], tiles(act32), ACT.Copy).then_inc(S("f2_hi"), 1)
                for _ in range(8):
                    hi()
                act.wait_ge(S("w_used"), pl.v + pl.ov - 4)
                act.activation(gtmp, acc[:, pl.g % 2], ACT.Relu).then_inc(S("f2_relu"), 1)
                for _ in range(4):
                    hi()
                pl.g += 2

            def second(n, downs):
                if downs:
                    for _ in range(4):
                        hi()
                act.wait_ge(S("w_used"), pl.v + pl.ov - (4 if downs else 0))
                act.wait_ge(S("f2_act"), 2 * n + 1)
                act.activation(gtmp, acc[:, (pl.g + 1) % 2], ACT.Relu).then_inc(S("f2_relu"), 1)
                if downs:
                    for _ in range(12):
                        hi()
                    pl.g += 4

            up(4, 0, False)
            second(0, False)
            with act.Fori(0, 7) as i:
                pl.enter(i, 32, 32, 6)
                up(0, i + 1, True)
                second(i + 1, True)
            pl.leave(7, 32, 32, 6)
            for _ in range(4):
                hi()
            act.wait_ge(S("w_used"), pl.v - 4)
            act.wait_ge(S("f2_act"), 16)
            act.activation(yH[:], tiles(act32), ACT.Copy).then_inc(S("f2_hi"), 1)
            for _ in range(12):
                hi()
            act.wait_ge(S("f2_sum"), 32)
            norm_stats(5, O32, tiles(blk(4, 2)))

        @block.tensor
        def _(pe):
            pl = Place()

            def mm(o, l, r, start, stop):
                return pe.matmul(o, l, r, start=start, stop=stop, skip_group_check=True)

            def group(units, xh, xl, free, mode="A", k0=0, ready=None, hooks={}):
                for name, value in free:
                    pe.wait_ge(S(name), value)
                a = acc[:, pl.g % 2]
                for u in range(units):
                    if ready:
                        ready(u)
                    pe.wait_ge(S("unit_done"), pl.u + pl.ou + 1)
                    for k in range(KU):
                        kt = k0 + u * KU + k
                        first, last = u == 0 and k == 0, u == units - 1 and k == KU - 1
                        wh = whi[:, pl.v % NSPLIT, k * GCOL:(k + 1) * GCOL]
                        wl = wlo[:, pl.v % NSPLIT, k * GCOL:(k + 1) * GCOL]
                        for m in range({"A": GT, "AB": 2, "B": 0}[mode]):
                            o, c = a[:, m * T:(m + 1) * T], slice(m * P, (m + 1) * P)
                            mm(o, wh[:, c], xh[:, kt], first and m % 2 == 0, False)
                            mm(o, wh[:, c], xl[:, kt], False, False)
                            ins = mm(o, wl[:, c], xh[:, kt], False, last)
                        for t in range({"A": 0, "AB": TT, "B": TT}[mode]):
                            n = T if mode == "AB" else GCOL
                            at = GCOL + t * n if mode == "AB" else t * n
                            o, c, tk = a[:, at:at + n], slice(GCOL - n, GCOL), slice(t * P, (t + 1) * P)
                            mm(o, xh[:, kt, tk], wh[:, c], first and (mode == "B" or t == 0), False)
                            mm(o, xl[:, kt, tk], wh[:, c], False, False)
                            ins = mm(o, xh[:, kt, tk], wl[:, c], False, last)
                    ins.then_inc(S("w_used"), 1)
                    pl.u += 1
                    pl.v += 1
                    if u in hooks:
                        hooks[u]()
                pl.g += 1

            def h_ready(index):
                def run(u):
                    if u % 2 == 0:
                        pe.wait_ge(S("h_lo"), 4 * index + u // 2 + 1)
                return run

            def norm_sum(k):
                pe.wait_ge(S("nm_red"), k + 1)
                mm(W[:, 3, 0:T], ones, red[:], True, True).then_inc(S("nm_sum"), 1)

            def level(l):
                def run():
                    if l == 0:
                        pe.wait_ge(S("f_in"), 2)
                        pe.wait_ge(S("q_in"), 2)
                    else:
                        pe.wait_ge(S("c_done"), l)
                        pe.wait_ge(S("st_in"), l)
                    a, b = (ka, qa) if l == 0 else (Cb, Cb)
                    if l < 8:
                        for j in range(2 * H):
                            c = slice(j * P, (j + 1) * P)
                            ins = mm(Wf[:, c], a[:, c], b[:, c], True, True)
                    else:
                        for h in range(H):
                            ins = mm(Wf[:, h * P:(h + 1) * P], Cb[:, h * T:h * T + P], Cb[:, h * T + P:(h + 1) * T],
                                     True, True)
                    ins.then_inc(S("lvl"), 1)
                return run

            def hgrn_out():
                pe.wait_ge(S("off_in"), 1)
                pe.wait_ge(S("i_in"), 2)
                for h in range(H):
                    c = slice(h * P, (h + 1) * P)
                    mm(Wf[:, h * T:h * T + P], iav[:, 0, c], ST[:, h * T:h * T + P], True, True)
                    o = Wf[:, h * T + P:(h + 1) * T]
                    mm(o, iav[:, 0, c], off[:, c], True, False)
                    ins = mm(o, iav[:, 1, c], ST[:, h * T + P:(h + 1) * T], False, True)
                ins.then_inc(S("o_mm"), 1)

            def head_sum(k):
                def run():
                    pe.wait_ge(S("hn_sq"), k + 1)
                    if k:
                        pe.wait_ge(S("hn_done"), k)
                    for j in range(2 * H):
                        ins = mm(W[:, 3, j:j + 1], Cb[:, j * P:(j + 1) * P], one, True, True)
                    ins.then_inc(S("hn_sum"), 1)
                return run

            def head_spread(k):
                def run():
                    pe.wait_ge(S("hn_rec"), k + 1)
                    for j in range(2 * H):
                        ins = mm(Wf[:, j * P:(j + 1) * P], rr[:, 1, j:j + 1].to_broadcast([P, P]), ident, True, True)
                    ins.then_inc(S("hn_bc"), 1)
                return run

            def att(n, n0, n1):
                if n0 <= n - 3 < n1:
                    m = n - 3
                    kind, q, k, vs, y, head, fst, lst, gt = jobs[m]
                    pe.wait_ge(S("att_pt"), m + 1)
                    if m < N_B:
                        pe.wait_ge(S("vb_in"), 2)
                    elif m < N_N:
                        pe.wait_ge(S("kv_in"), 3)
                    else:
                        pe.wait_ge(S("vm_in"), 2)
                    if fst and head >= 2:
                        pe.wait_ge(S("att_y"), head - 1)
                    pt = pt2[:, m % 2]
                    o = W[:, 3, (head % 2) * T:(head % 2 + 1) * T]
                    ins = mm(o, vs[0], pt[:, 0:T], fst, False)
                    if len(vs) > 1:
                        ins = mm(o[:, P:T], vs[1], pt[:, T:3 * P], False, lst)
                    ins.then_inc(S("att_pv"), 1)
                if n0 <= n - 2 < n1:
                    m = n - 2
                    pe.wait_ge(S("att_p"), m + 1)
                    if m == N_B:
                        pe.wait_ge(S("gates_in"), 1)
                    elif m:
                        pe.wait_ge(S("att_pt"), m)
                    for j in range(parts(jobs[m][0])[1][1] // P):
                        ins = pe.transpose(W[:, 2, j * P:(j + 1) * P], sb3[:, m % 3, j * P:(j + 1) * P], ident)
                    ins.then_inc(S("att_t"), 1)
                if n0 <= n < n1:
                    kind, q, k = jobs[n][:3]
                    if n == 0:
                        pe.wait_ge(S("hn_done"), 3)
                        pe.wait_ge(S("hk_in"), 16)
                    elif n >= N_N:
                        pe.wait_ge(S("roped"), 15)
                    elif kind == "cmp":
                        pe.wait_ge(S("kvc_in"), 1)
                    elif n >= N_B:
                        pe.wait_ge(S("roped"), 6 if n == N_B else 7)
                        pe.wait_ge(S("kvc_in"), 1)
                    if n >= 2:
                        pe.wait_ge(S("att_max"), n - 1)
                    s = W[:, n % 2]
                    for t, (a, b) in enumerate(parts(kind)):
                        w = b - a
                        if kind == "bias":
                            hk = HK[:, jobs[n][5] * T + (P if t == 0 else 0):][:, 0:w]
                            mm(s[:, a:b], flip, hk, True, False)
                        ins = mm(s[:, a:b], q[:, t * P:(t + 1) * P], k[:, 0:w], kind != "bias", True)
                    ins.then_inc(S("att_s"), 1)

            def slot(n, n0, n1):
                return lambda: att(n, n0, n1)

            def also(*fs):
                return lambda: [f() for f in fs]

            def ada_sum(a):
                pe.wait_ge(S("unit_done"), pl.u + pl.ou)
                for m in range(GT):
                    o = modP[:, ds(a * GT + m, 1)] if not isinstance(a, int) else modP[:, a * GT + m:a * GT + m + 1]
                    for e in range(2):
                        ins = mm(o, adaacc[:, pl.a % 2, e, m * P:(m + 1) * P], one, e == 0, e == 1)
                ins.then_inc(S("ada_sum"), 1)
                pl.a += 1

            pe.wait_ge(S("x_in"), 64)
            norm_sum(0)
            group(8, hH, hL, (), ready=h_ready(0))
            group(8, hH, hL, ())
            group(8, hH, hL, (("sig_f", 1),))
            group(8, hH, hL, (("sig_f", 2),))
            group(8, hH, hL, (("q_in", 1),), "B")
            group(8, hH, hL, (("q_in", 2),), "B")
            group(8, hH, hL, (("i_in", 1),), hooks={6: level(0)})
            group(8, hH, hL, (("i_in", 2),), hooks={6: level(1)})
            group(8, hH, hL, (("g_in", 1),), hooks={6: level(2)})
            group(8, hH, hL, (("g_in", 2),), hooks={6: level(3)})
            group(8, hH, hL, (("qk_in", 1),), hooks={6: level(4)})
            group(8, hH, hL, (("qk_in", 2),), hooks={6: level(5)})
            group(8, hH, hL, (("qk_in", 3),), "B", hooks={6: level(6)})
            group(8, hH, hL, (("qk_in", 4),), "B", hooks={6: level(7)})
            group(8, hH, hL, (("vb_in", 1),), hooks={6: level(8)})
            group(8, hH, hL, (("vb_in", 2),), hooks={1: hgrn_out, 4: head_sum(0), 7: head_spread(0)})
            group(8, hH, hL, (("gate_in", 1),), hooks={1: head_sum(1), 4: head_spread(1), 6: head_sum(2)})
            group(8, hH, hL, (("gate_in", 2),), hooks={1: head_spread(2), 7: slot(0, 0, N_B)})

            def y_ready(index):
                def run(u):
                    if u == 0:
                        pe.wait_ge(S("y_lo"), index)
                return run
            for i in range(4):
                group(4, yH, yL, (("gate_in", 3 + i) if i < 2 else ("pa_in", i - 1),), ready=y_ready(1),
                      hooks={3: slot(i + 1, 0, N_B)})
            for i in range(4):
                group(8, hH, hL, (("pa_in", 3 + i) if i < 2 else ("gate_in", 5 + i - 2),),
                      hooks={3: slot(5 + 2 * i, 0, N_B), 7: slot(6 + 2 * i, 0, N_B)})
            for i in range(4):
                group(4, yH, yL, (("gate_in", 7 + i) if i < 2 else ("pb_in", i - 1),), ready=y_ready(2))

            def merged_ready(u):
                if u % 2 == 0:
                    pe.wait_ge(S("m_lo"), u // 2 + 1)
            for i in range(4):
                pl.u += 4
                group(8, hH, hL, (("pb_in", 3 + i) if i < 2 else ("x1", i - 1),), ready=merged_ready)
                if i % 2:
                    ada_sum(i // 2)

            norm_sum(1)

            def ffn1(n, free, down):
                group(8, hH, hL, free[0:1], ready=None if down else h_ready(1))
                pl.u += 8
                group(8, hH, hL, free[1:2])
                ada_sum(2 * n + 2)
                pl.u += 8
                if down:
                    down1(n, (("ff_g", n + 1), ("ff_act", n + 1)))
                ada_sum(2 * n + 3)

            def down1(n, free):
                pe.wait_ge(S("ff_lo"), n)
                for g in range(4):
                    group(2, yH, yL, free[g:g + 1] if g < 2 else (("ff_sum", (n - 1) * 4 + g - 1),))

            ffn1(0, (("x1", 3), ("x1", 4)), False)
            ffn1(1, (("ff_g", 1), ("ff_act", 1)), True)
            with pe.Fori(0, 9) as i:
                pl.enter(i, 40, 24, 6, 2)
                ffn1(i + 2, (("ff_sum", i * 4 + 3), ("ff_sum", i * 4 + 4)), True)
            pl.leave(9, 40, 24, 6, 2)
            down1(11, (("ff_sum", 39), ("ff_sum", 40)))

            norm_sum(2)

            def rotate(n, g, c0):
                def run():
                    pe.wait_ge(S("rope_raw"), n + 1)
                    mm(acc[:, g % 2, c0:c0 + GCOL], swap, rope, True, True).then_inc(S("rope_swap"), 1)
                return run
            gg = PHASES["cmp_kv"][2]
            group(8, hH, hL, (("ff_sum", 43),), ready=h_ready(2))
            group(8, hH, hL, (("ff_sum", 44),), hooks={2: rotate(0, gg, 0)})
            group(8, hH, hL, (("roped", 1), ("kv_in", 1)), hooks={2: rotate(1, gg + 1, 0), 5: rotate(2, gg + 1, GCOL)})
            for kind in range(2):
                pe.wait_ge(S("cx_lo"), kind + 1)
                xs = [y[:].rearrange("p a b -> p (a b)")[:, kind * 1024:kind * 1024 + 960] for y in (yH, yL)]
                for u in range(4):
                    pe.wait_ge(S("unit_done"), pl.u + 1)
                    for k in range(8):
                        c, x = slice(k * P, (k + 1) * P), slice((u * 8 + k) * 30, (u * 8 + k + 1) * 30)
                        o = hidP[:, kind, 0:30]
                        wh, wl = whi[:, pl.v % NSPLIT, c], wlo[:, pl.v % NSPLIT, c]
                        mm(o, wh, xs[0][:, x], u == 0 and k == 0, False)
                        mm(o, wh, xs[1][:, x], False, False)
                        ins = mm(o, wl, xs[0][:, x], False, u == 3 and k == 7)
                    ins.then_inc(S("w_used"), 1)
                    pl.u += 1
                    pl.v += 1
                    if (kind, u) == (0, 2):
                        rotate(3, gg + 2, 0)()
                    if (kind, u) == (1, 1):
                        rotate(4, gg + 2, GCOL)()

            def gates_mm():
                pe.wait_ge(S("wg_lo"), 1)
                for t in range(TT):
                    o, tk = W[:, 2, t * N_GATE:(t + 1) * N_GATE], slice(t * P, (t + 1) * P)
                    for k in range(KT):
                        mm(o, hH[:, k, tk], wgh[:, k], k == 0, False)
                        mm(o, hL[:, k, tk], wgh[:, k], False, False)
                        ins = mm(o, hH[:, k, tk], wgl[:, k], False, k == KT - 1)
                ins.then_inc(S("gates_mm"), 1)

            def compressed():
                pe.wait_ge(S("hid_in"), 1)
                mm(W[:, 0, 0:T], w2[:, 0], hid[:, 0].rearrange("p g c -> p (g c)"), True, True)
                for g in range(2):
                    ins = mm(W[:, 0, T + g * P:T + (g + 1) * P], hid[:, 1, g], w2[:, 1], True, True)
                ins.then_inc(S("cmp_kv"), 1)
            group(8, hH, hL, (("roped", 3),), "AB", hooks={0: gates_mm, 3: compressed})
            group(8, hH, hL, (("roped", 5),), "AB", hooks={2: rotate(5, gg + 3, 0)})
            n = N_B
            frees = ((("roped", 6), ("kv_in", 2)), (("roped", 7), ("kv_in", 3)), (("roped", 9),), (("roped", 11),),
                     (("roped", 13),), (("roped", 15),))
            for j in range(6):
                hooks = {}
                for u in ((0, 3, 4, 6) if j == 0 else (0, 2, 4, 6)):
                    hooks[u] = slot(n, N_B, N_N)
                    n += 1
                if j == 5:
                    for u in (5, 6, 7):
                        hooks[u] = slot(n - 1, N_B, N_N)
                        n += 1
                    n -= 1
                    hooks[7] = also(hooks[7], slot(n, N_B, N_N))
                if j == 0:
                    hooks[2] = rotate(6, gg + 4, 0)
                elif j <= 4:
                    r = 7 + 2 * (j - 1)
                    first = rotate(r, gg + 4 + j, 0)
                    hooks[2] = also(first, hooks[2])
                    hooks[5] = rotate(r + 1, gg + 4 + j, GCOL)
                group(8, hH, hL, frees[j], "B" if j >= 4 else "A", hooks=hooks)
            assert n == N_N + 2
            n = N_N
            frees = (("vm_in", 1), ("vm_in", 2), ("wo_in", 1), ("wo_in", 2))
            for i, at in enumerate(((2, 3), (0, 2, 3), (0, 2, 3), (0, 2, 3))):
                hooks = {}
                for u in at:
                    hooks[u] = slot(n, N_N, N_M)
                    n += 1
                group(4, yH, yL, frees[i:i + 1], ready=y_ready(3), hooks=hooks)
            assert n == N_M + 3
            frees = (("wo_in", 3), ("wo_in", 4), ("o_sum", 1), ("o_sum", 2))

            def om_ready(u):
                if u == 0:
                    pe.wait_ge(S("om_lo"), 1)
            for i in range(4):
                group(4, hH, hL, frees[i:i + 1], ready=om_ready)
            norm_sum(3)
            norm_sum(4)

            def down2(n, free):
                pe.wait_ge(S("f2_lo"), n)
                for g in range(4):
                    group(4, yH, yL, free[g:g + 1] if g < 2 else (("f2_sum", (n - 1) * 4 + g - 1),))

            def ffn2(n, free, down):
                group(8, hH, hL, free[0:1], ready=None if down else h_ready(3))
                group(8, hH, hL, free[1:2])
                if down:
                    down2(n, (("f2_relu", 2 * n + 1), ("f2_relu", 2 * n + 2)))

            ffn2(0, (("o_sum", 3), ("o_sum", 4)), False)
            ffn2(1, (("f2_relu", 1), ("f2_relu", 2)), True)
            with pe.Fori(0, 6) as i:
                pl.enter(i, 32, 32, 6)
                ffn2(i + 2, (("f2_sum", i * 4 + 3), ("f2_sum", i * 4 + 4)), True)
            pl.leave(6, 32, 32, 6)
            down2(8, (("f2_sum", 27), ("f2_sum", 28)))
            norm_sum(5)

        @block.vector
        def _(dve):
            pl = Place()
            steps = [0]

            def then(ins):
                steps[0] += 1
                ins.then_inc(S("dve_step"), 1)
                dve.wait_ge(S("dve_step"), steps[0])

            def lo(n=1):
                for _ in range(n):
                    s, v = pl.u % NRAW, pl.v % NSPLIT
                    dve.wait_ge(S("w_hi"), pl.v + pl.ov + 1)
                    dve.tensor_tensor(wlo[:, v], raw[:, s], whi[:, v].bitcast(F32), ALU.subtract)\
                       .then_inc(S("unit_done"), 1)
                    pl.u += 1
                    pl.v += 1

            def group(units=8, hooks={}, begin=0):
                for u in range(begin, units):
                    lo()
                    if u in hooks:
                        hooks[u]()
                pl.g += 1

            def norm_rstd(k, sq):
                dve.wait_ge(S("nm_sq"), k + 1)
                dve.tensor_reduce(red[:], sq.rearrange("p k t -> p t k"), AX.X, ALU.add).then_inc(S("nm_red"), 1)
                dve.wait_ge(S("nm_root"), k + 1)
                then(dve.reciprocal(rstd[:], rstd[:]))

            def h_low(index, h32, c):
                dve.wait_ge(S("h_hi"), 4 * index + c + 1)
                q = slice(4 * c, 4 * c + 4)
                dve.tensor_tensor(hL[:, q], h32[:, q], hH[:, q].bitcast(F32), ALU.subtract).then_inc(S("h_lo"), 1)

            def norm_h(index, x, h32, gain):
                for c in range(4):
                    for j in range(4 * c, 4 * c + 4):
                        ins = dve.scalar_tensor_tensor(out=h32[:, j], in0=x[:, j], scalar=V(gain, 1, j), in1=rstd[:],
                                                       op0=ALU.mult, op1=ALU.mult)
                    ins.then_inc(S("h_ready"), 1)
                    if c:
                        h_low(index, h32, c - 1)
                h_low(index, h32, 3)

            def modulated_h(index, x, h32, a, shift):
                for c in range(4):
                    q = slice(4 * c, 4 * c + 4)
                    then(dve.tensor_tensor(h32[:, q], x[:, q], rstd[:].unsqueeze(1).to_broadcast([P, 4, T]), ALU.mult))
                    for j in range(4 * c, 4 * c + 4):
                        ins = dve.tensor_scalar(h32[:, j], h32[:, j], modA[:, a, j:j + 1],
                                                mod[:, shift + j:shift + j + 1], ALU.mult, ALU.add)
                    ins.then_inc(S("h_ready"), 1)
                    if c:
                        h_low(index, h32, c - 1)
                h_low(index, h32, 3)

            dve.wait_ge(S("ext_in"), 16)
            dve.tensor_copy(ext[:, 0:P], ext[:, P:P + 1].to_broadcast([H, P])).then_inc(S("ext_full"), 1)
            e = P + N_REL
            dve.tensor_copy(ext[:, e:EXT], ext[:, e - 1:e].to_broadcast([H, EXT - e])).then_inc(S("ext_full"), 1)
            dve.wait_ge(S("x_in"), 64)
            then(dve.tensor_copy(lmask[:], lmaskf))
            l0, l1 = V("lb", H), V("lb", H, H)
            then(dve.tensor_tensor(lb[:, 2], l0, l1, ALU.max))
            dve.tensor_tensor(lb[:, 0], l0, lb[:, 2], ALU.subtract)
            dve.tensor_tensor(lb[:, 1], l1, lb[:, 2], ALU.subtract).then_inc(S("lb_step"), 1)
            then(dve.tensor_scalar(small[:, 0:1], V("q_gain"), SCALE, None, ALU.mult))
            dve.wait_ge(S("lb_exp"), 1)
            then(dve.tensor_tensor(lb[:, 2], lb[:, 0], lb[:, 1], ALU.add))
            then(dve.reciprocal(lb[:, 3], lb[:, 2]))
            then(dve.tensor_tensor(lb[:, 4], lb[:, 0], lb[:, 3], ALU.mult))
            then(dve.tensor_scalar(lb[:, 5], lb[:, 4], -1.0, 1.0, ALU.mult, ALU.add))
            dve.wait_ge(S("c_sig"), 1)
            then(dve.tensor_tensor(cs[:], cs[:], V("c", 16), ALU.mult))
            lo(4)
            norm_rstd(0, sq0)
            norm_h(0, x0, sq0, "norm_mix")

            def half(b, i):
                return b[:, i * 1024:(i + 1) * 1024]

            def forget(i):
                def run():
                    dve.wait_ge(S("sig_f"), i + 1)
                    for h in range(4 * i, 4 * i + 4):
                        c = slice(h * T, (h + 1) * T)
                        ins = dve.tensor_scalar(Cb[:, c], ka[:, c], lb[:, 5, h:h + 1], lb[:, 4, h:h + 1],
                                                ALU.mult, ALU.add)
                    then(ins)
                    dve.tensor_scalar(half(ka, i), half(Cb, i), -1.0, 1.0, ALU.mult, ALU.add)
                    dve.tensor_scalar(half(Cb, i), half(Cb, i), 2.0 ** -63, None, ALU.max).then_inc(S("f_in"), 1)
                return run

            def silu_q(i):
                def run():
                    dve.wait_ge(S("sig_q"), i + 1)
                    dve.tensor_tensor(half(qa, i), half(qa, i), acc[:, (2 + i) % 2], ALU.mult).then_inc(S("q_in"), 1)
                return run

            def silu_g(i):
                def run():
                    dve.wait_ge(S("sig_g"), i + 1)
                    for h in range(4):
                        c = slice((4 * i + h) * T, (4 * i + h + 1) * T)
                        ins = dve.scalar_tensor_tensor(out=ga[:, c], in0=ga[:, c], scalar=V("out_gain", 1, 4 * i + h),
                                                       in1=acc[:, (6 + i) % 2, h * T:(h + 1) * T],
                                                       op0=ALU.mult, op1=ALU.mult)
                    ins.then_inc(S("g_in"), 1)
                return run

            def scan():
                dve.wait_ge(S("ln_f"), 1)
                for j in range(2 * H):
                    c = slice(j * P, (j + 1) * P)
                    ins = dve.tensor_tensor_scan(bc[:, c], ones, Cb[:, c], 0.0, ALU.mult, ALU.add)
                then(ins)

            def take(l):
                dve.wait_ge(S("lvl"), l + 1)
                if l == 0:
                    dve.wait_ge(S("st_zero"), 1)
                mask = lmask[:, l * P:(l + 1) * P].unsqueeze(1).to_broadcast([P, 2 * H, P])
                dve.copy_predicated(ST.rearrange("p (j t) -> p j t", t=P), mask, Wf.rearrange("p (j t) -> p j t", t=P))\
                   .then_inc(S("st_in"), 1)

            def diff(l):
                if l < 8:
                    b = 1 << (l - 1)
                    v = bc.rearrange("p (n b) -> p n b", b=2 * b)
                    dve.tensor_tensor(Cb.rearrange("p (n b) -> p n b", b=2 * b), v,
                                      v[:, :, b - 1:b].to_broadcast([P, BLK // (2 * b), 2 * b]), ALU.subtract)\
                       .then_inc(S("c_diff"), 1)
                else:
                    v = bc.rearrange("p (h t s) -> p h t s", h=H, t=TT)[:, :, 0]
                    dve.tensor_tensor(Cb.rearrange("p (h t s) -> p h t s", h=H, t=TT)[:, :, 0], v,
                                      v[:, :, P - 1:P].to_broadcast([P, H, P]), ALU.subtract).then_inc(S("c_diff"), 1)

            def prepare(l):
                def run():
                    take(l - 1)
                    diff(l)
                return run

            def decayed(l):
                def run():
                    dve.wait_ge(S("c_exp"), l)
                    b = 1 << (l - 1) if l < 8 else P
                    v, kv, qv = (x.rearrange("p (n h b) -> p n h b", h=2, b=b) for x in (Cb, ka, qa))
                    dve.tensor_tensor(v[:, :, 0], v[:, :, 0], kv[:, :, 0], ALU.mult)
                    dve.tensor_tensor(v[:, :, 1], v[:, :, 1], qv[:, :, 1], ALU.mult).then_inc(S("c_done"), 1)
                return run

            group(begin=4)
            group(hooks={5: forget(0)})
            group(hooks={5: forget(1)})
            group(hooks={5: silu_q(0)})
            group(hooks={5: silu_q(1)})
            group(hooks={3: scan})
            group()
            group(hooks={4: silu_g(0), 5: prepare(1), 7: decayed(1)})
            group(hooks={4: silu_g(1), 5: prepare(2), 7: decayed(2)})
            for l in range(3, 9):
                group(hooks={5: prepare(l), 7: decayed(l)})

            def head_rec(k):
                def run():
                    dve.wait_ge(S("hn_root"), k + 1)
                    dve.reciprocal(rr[:, 1], rr[:, 0]).then_inc(S("hn_rec"), 1)
                return run

            def head_apply(k):
                def run():
                    if k == 0:
                        dve.wait_ge(S("o_in"), 1)
                        dve.wait_ge(S("hn_sq"), 1)
                        then(dve.tensor_tensor(ob, ob, ga, ALU.mult))
                        dve.wait_ge(S("hn_bc"), 1)
                        dve.tensor_tensor(ob, ob, Wf, ALU.mult).then_inc(S("hn_done"), 1)
                    else:
                        x, g = ((qb, small[:, 0:1]), (kb, V("k_gain")))[k - 1]
                        dve.wait_ge(S("hn_bc"), k + 1)
                        dve.scalar_tensor_tensor(out=x, in0=x, scalar=g, in1=Wf, op0=ALU.mult, op1=ALU.mult)\
                           .then_inc(S("hn_done"), 1)
                return run

            def y_low(n, src):
                dve.wait_ge(S("y_hi"), n)
                dve.tensor_tensor(yL[:], tiles(src), yH[:].bitcast(F32), ALU.subtract).then_inc(S("y_lo"), 1)

            def also(*fs):
                return lambda: [f() for f in fs]

            group()
            group(hooks={0: head_rec(0), 3: head_apply(0), 5: also(lambda: y_low(1, ob), head_rec(1))})
            group(hooks={0: head_apply(1), 2: head_rec(2), 5: head_apply(2)})

            def att(n, n0, n1):
                if n0 <= n - 1 < n1:
                    m = n - 1
                    kind, gt = jobs[m][0], jobs[m][8]
                    r = m % 3
                    dve.wait_ge(S("att_exp"), m + 1)
                    then(dve.tensor_scalar(stat[:, 3, r], stat[:, 2, r], TINY, None, ALU.max))
                    then(dve.reciprocal(stat[:, 3, r], stat[:, 3, r]))
                    if m == N_B:
                        dve.wait_ge(S("gates_in"), 1)
                    for t, (a, b) in enumerate(parts(kind)):
                        p, s = sb3[:, r, a:b], stat[:, 3, r, t:t + 1]
                        if gt:
                            ins = dve.tensor_scalar(p, p, s, gt[t], ALU.mult, ALU.mult)
                        else:
                            ins = dve.tensor_scalar(p, p, s, None, ALU.mult)
                    ins.then_inc(S("att_p"), 1)
                if n0 <= n < n1:
                    kind, r = jobs[n][0], n % 3
                    dve.wait_ge(S("att_s"), n + 1)
                    if n >= 3:
                        dve.wait_ge(S("att_t"), n - 2)
                    for t, (a, b) in enumerate(parts(kind)):
                        ins = dve.tensor_tensor_reduce(sb3[:, r, a:b], W[:, n % 2, a:b], mask_of(kind, t), 1.0,
                                                       MAX_FLOOR, ALU.add, ALU.max, stat[:, 0, r, t:t + 1])
                    ins.then_inc(S("att_max"), 1)
                    dve.wait_ge(S("att_max"), n + 1)
                    dve.tensor_scalar(stat[:, 1, r], stat[:, 0, r], -1.0 if kind == "bias" else -SCALE, None, ALU.mult)\
                       .then_inc(S("att_neg"), 1)

            def slot(n, n0, n1):
                return lambda: att(n, n0, n1)

            def by_gate_a(i):
                def run():
                    m = half(M, i)
                    dve.wait_ge(S("gate_in"), i + 1)
                    dve.wait_ge(S("w_used"), PHASES["proj_a"][1] + 4 * (i + 1))
                    dve.tensor_tensor(m, m, acc[:, (PHASES["proj_a"][2] + i) % 2], ALU.mult).then_inc(S("pa_in"), 1)
                return run

            def by_gate_b(i):
                def run():
                    g = half(sgb, i)
                    dve.wait_ge(S("gate_in"), i + 5)
                    dve.wait_ge(S("w_used"), PHASES["proj_b"][1] + 4 * (i + 1))
                    dve.tensor_tensor(g, g, acc[:, (PHASES["proj_b"][2] + i) % 2], ALU.mult).then_inc(S("pb_in"), 1)
                    dve.wait_ge(S("pb_in"), i + 1)
                    dve.wait_ge(S("pa_in"), i + 1)
                    dve.tensor_tensor(half(M, i), half(M, i), g, ALU.add).then_inc(S("merged"), 1)
                return run

            group(4, hooks={2: slot(0, 0, N_B)})
            for i in range(1, 4):
                group(4, hooks={2: slot(i, 0, N_B), 3: by_gate_a(i - 1)})
            for i in range(4):
                hooks = {2: slot(4 + 2 * i, 0, N_B), 6: slot(5 + 2 * i, 0, N_B)}
                if i == 0:
                    hooks[3] = by_gate_a(3)
                group(hooks=hooks)
            group(4, hooks={3: lambda: y_low(2, yb)})
            for i in range(1, 4):
                group(4, hooks={3: by_gate_b(i - 1)})

            def ada_unit(j):
                s = pl.u % NRAW
                dve.wait_ge(landed[s], 16 * (pl.u // NRAW + 1) + pl.ou * (16 // NRAW))
                for e in range(2):
                    w, c, o = raw[:, s, e * GCOL:(e + 1) * GCOL], cs[:, 2 * j + e:2 * j + e + 1], adaacc[:, pl.a % 2, e]
                    if j == 0:
                        if e == 0 and pl.a >= 2:
                            dve.wait_ge(S("ada_sum"), pl.a + pl.oa - 1)
                        ins = dve.tensor_scalar(o, w, c, None, ALU.mult)
                    else:
                        if e == 0:
                            dve.wait_ge(S("ada_even"), pl.a * 8 + j + pl.oa * 8)
                        else:
                            dve.wait_ge(S("unit_done"), pl.u + pl.ou)
                        ins = dve.scalar_tensor_tensor(out=o, in0=w, scalar=c, in1=o, op0=ALU.mult, op1=ALU.add)
                    ins.then_inc(S("unit_done") if e else S("ada_even"), 1)
                pl.u += 1

            def ada(begin, end):
                for j in range(begin, end):
                    ada_unit(j)
                if end == 8:
                    pl.a += 1

            def merged_low(c):
                q = slice(4 * c, 4 * c + 4)
                dve.wait_ge(S("m_hi"), c + 1)
                dve.tensor_tensor(hL[:, q], tiles(M)[:, q], hH[:, q].bitcast(F32), ALU.subtract).then_inc(S("m_lo"), 1)

            def add_x(i):
                def run():
                    if i == 0:
                        dve.wait_ge(S("x_again"), 16)
                    dve.wait_ge(S("w_used"), PHASES["out"][1] + 8 * (i + 1))
                    x = X[:, 4 * i:4 * i + 4]
                    dve.tensor_tensor(x, x, tiles(acc[:, (PHASES["out"][2] + i) % 2]), ALU.add).then_inc(S("x1"), 1)
                return run
            ada(0, 4)
            lo(4)
            by_gate_b(3)()
            for c in range(4):
                merged_low(c)
            lo(4)
            pl.g += 1
            for i in range(1, 4):
                ada(4 * (i % 2), 4 * (i % 2) + 4)
                group(hooks={3: add_x(i - 1)})
            lo(4)
            add_x(3)()
            norm_rstd(1, tiles(M))
            norm_h(1, X, tiles(M), "norm_ffn")

            def product_low(n):
                dve.wait_ge(S("ff_hi"), n)
                dve.tensor_tensor(yL[:, 0:GT], tiles(act32[:, 0:1024]), yH[:, 0:GT].bitcast(F32), ALU.subtract)\
                   .then_inc(S("ff_lo"), 1)

            def add_down(g, n, v):
                dve.wait_ge(S("w_used"), v)
                dve.wait_ge(S("ff_sum"), (n - 1) * 4 + g) if not isinstance(n, int) or (n - 1) * 4 + g > 0 else None
                x = X[:, 4 * g:4 * g + 4]
                dve.tensor_tensor(x, x, tiles(acc[:, (PHASES["ffn1"][2] + g) % 2]), ALU.add).then_inc(S("ff_sum"), 1)

            def ffn1(n, begin, before, down):
                here = lambda: pl.v + pl.ov
                if before:
                    lo(2)
                    add_down(2, n - 1, here() - 4)
                    lo(2)
                    add_down(3, n - 1, here() - 4)
                    product_low(n)
                    lo(4)
                else:
                    if down:
                        lo(4)
                        product_low(n)
                        lo(4)
                    else:
                        lo(8 - begin)
                ada(0, 8)
                lo(4)
                dve.wait_ge(S("ff_sig"), n + 1)
                dve.tensor_tensor(gtmp, gtmp, acc[:, PHASES["ffn1"][2] % 2], ALU.mult).then_inc(S("ff_g"), 1)
                lo(4)
                ada(0, 8)
                if down:
                    lo(4)
                dve.wait_ge(S("w_used"), here() - (4 if down else 0))
                dve.wait_ge(S("ff_g"), n + 1)
                dve.tensor_tensor(act32[:, 0:1024], gtmp, acc[:, (PHASES["ffn1"][2] + 1) % 2], ALU.mult)\
                   .then_inc(S("ff_act"), 1)
                if down:
                    lo(2)
                    add_down(0, n, here() - 4)
                    lo(2)
                    add_down(1, n, here() - 4)

            ffn1(0, 4, False, False)
            ffn1(1, 0, False, True)
            with dve.Fori(0, 9) as i:
                pl.enter(i, 40, 24, 6, 2)
                ffn1(i + 2, 0, True, True)
            pl.leave(9, 40, 24, 6, 2)
            lo(2)
            add_down(2, 10, pl.v - 4)
            lo(2)
            add_down(3, 10, pl.v - 4)
            product_low(11)
            lo(2)
            add_down(0, 11, pl.v - 4)
            lo(2)
            add_down(1, 11, pl.v - 4)
            dve.wait_ge(S("ada_sum"), 24)
            then(dve.tensor_tensor(mod[:], modP, V("b_ada", 96), ALU.add))
            for a, (scale, add, gain) in enumerate(((16, 1.0, "pre_mix"), (32, 0.0, "post_mix"), (64, 1.0, "pre_ffn"),
                                                    (80, 0.0, "post_ffn"))):
                ins = dve.scalar_tensor_tensor(out=modA[:, a], in0=mod[:, scale:scale + 16], scalar=add,
                                               in1=V(gain, 16), op0=ALU.add, op1=ALU.mult)
            then(ins)
            lo(2)
            add_down(2, 11, pl.v - 4)
            lo(2)
            add_down(3, 11, pl.v - 4)
            norm_rstd(2, O32)
            modulated_h(2, X, O32, 0, 0)
            dve.wait_ge(S("wg_hi"), 1)
            dve.tensor_tensor(wgl[:], wg, wgh[:].bitcast(F32), ALU.subtract).then_inc(S("wg_lo"), 1)

            def rotated(n, g, c0, dst):
                def run():
                    tab = lambda name: C(name, T).unsqueeze(1).to_broadcast([P, 2, T])
                    r, d = tiles(rope), tiles(dst)
                    dve.wait_ge(S("rope_swap"), n + 1)
                    then(dve.tensor_tensor(d, r, tab("cos"), ALU.mult))
                    then(dve.tensor_tensor(r, tiles(acc[:, g % 2, c0:c0 + GCOL]), tab("sin"), ALU.mult))
                    dve.tensor_tensor(d, d, r, ALU.add).then_inc(S("roped"), 1)
                return run

            def blocks(kind):
                def run():
                    if kind == 0:
                        dve.wait_ge(S("roped"), 1)
                    else:
                        dve.wait_ge(S("kv_in"), 1)
                    base = arena[:, 0:1]
                    src = bass.AP(base.tensor, base.offset + kind * 2 * T,
                                  [list(base.ap[0]), [1, CMP_LEN], [T, 2], [CMP_STRIDE, N_CMP]])
                    pos = V("v_pos" if kind else "k_pos", CMP_LEN)
                    pos = bass.AP(pos.tensor, pos.offset, [list(pos.ap[0]), [1, CMP_LEN], [0, 2], [0, N_CMP]])
                    o = cx[:, kind * 1024:kind * 1024 + 960].rearrange("p (l g c) -> p l g c", g=2, c=N_CMP)
                    dve.tensor_tensor(o, src, pos, ALU.add).then_inc(S("cx"), 1)
                return run

            def blocks_low(kind):
                def run():
                    c = slice(kind * 1024, kind * 1024 + 960)
                    y = lambda t: t[:].rearrange("p a b -> p (a b)")[:, c]
                    dve.wait_ge(S("cx_hi"), kind + 1)
                    dve.tensor_tensor(y(yL), cx[:, c], y(yH).bitcast(F32), ALU.subtract).then_inc(S("cx_lo"), 1)
                return run

            def hidden():
                dve.wait_ge(S("hid_sig"), 1)
                dve.wait_ge(S("hid_zero"), 1)
                for k in range(2):
                    g = lambda x: x.rearrange("p (g c) -> p g c", g=2)
                    ins = dve.tensor_tensor(hid[:, k, :, 0:N_CMP], g(hsg[:, k, 0:30]), g(hidP[:, k, 0:30]), ALU.mult)
                ins.then_inc(S("hid_in"), 1)

            gg = PHASES["cmp_kv"][2]
            group(begin=4)
            group(hooks={5: rotated(0, gg, 0, arena[:, 0:GCOL])})
            group(hooks={1: blocks(0), 2: blocks(1), 5: rotated(1, gg + 1, 0, qn[:, 0:GCOL]),
                         6: blocks_low(0), 7: blocks_low(1)})
            lo(1)
            rotated(2, gg + 1, GCOL, qn[:, GCOL:2 * GCOL])()
            lo(5)
            rotated(3, gg + 2, 0, qn[:, 2 * GCOL:3 * GCOL])()
            lo(2)
            group(hooks={0: rotated(4, gg + 2, GCOL, qn[:, 3 * GCOL:4 * GCOL]), 5: hidden})
            group(hooks={5: rotated(5, gg + 3, 0, arena[:, 1024:1536])})
            n = N_B
            dst = [qm[:, i * GCOL:(i + 1) * GCOL] for i in range(4)] + [km[:, i * GCOL:(i + 1) * GCOL] for i in range(4)]
            for j in range(6):
                hooks = {}
                for u in ((3, 6, 7) if j == 0 else (1, 3, 5, 7)):
                    hooks[u] = slot(n, N_B, N_N)
                    n += 1
                if j == 0:
                    hooks[4] = rotated(6, gg + 4, 0, arena[:, 1536:2048])
                else:
                    r = 7 + 2 * (j - 1)
                    if j <= 4:
                        hooks[5] = also(rotated(r, gg + 4 + j, 0, dst[r - 7]), hooks[5])
                    if j >= 2:
                        hooks[0] = rotated(r - 1, gg + 3 + j, GCOL, dst[r - 8])
                group(hooks=hooks)
            for u in range(4):
                lo(1)
                att(n + u, N_B, N_N)
            y_low(3, on)
            pl.g += 1
            n = N_N
            for i in range(1, 4):
                group(4, hooks={1: slot(n, N_N, N_M), 2: slot(n + 1, N_N, N_M), 3: slot(n + 2, N_N, N_M)})
                n += 3
            lo(2)
            att(n, N_N, N_M)
            lo(2)
            att(n + 1, N_N, N_M)
            dve.wait_ge(S("om_hi"), 1)
            dve.tensor_tensor(hL[:, 0:8], tiles(om), hH[:, 0:8].bitcast(F32), ALU.subtract).then_inc(S("om_lo"), 1)
            pl.g += 1

            def wo_add(i):
                def run():
                    dve.wait_ge(S("wo_in"), i + 1)
                    dve.wait_ge(S("w_used"), PHASES["wo"][1] + 16 + 4 * (i + 1))
                    o = O32[:, 4 * i:4 * i + 4]
                    dve.tensor_tensor(o, o, tiles(acc[:, (PHASES["wo"][2] + i) % 2]), ALU.add).then_inc(S("o_sum"), 1)
                return run
            for i in range(1, 4):
                group(4, hooks={3: wo_add(i - 1)})
            lo(4)
            wo_add(3)()

            def post_norm(k, a, sem, sq):
                norm_rstd(k, sq)
                for j in range(KT):
                    ins = dve.scalar_tensor_tensor(out=O32[:, j], in0=O32[:, j], scalar=modA[:, a, j:j + 1], in1=rstd[:],
                                                   op0=ALU.mult, op1=ALU.mult)
                then(ins)
                dve.tensor_tensor(X, X, O32, ALU.add).then_inc(S(sem), 1)
                dve.wait_ge(S(sem), 1)
            post_norm(3, 1, "x_mix", tiles(blk(4, 2)))
            norm_rstd(4, O32)
            modulated_h(3, X, O32, 2, 48)

            def square(n):
                i = n[0]
                dve.wait_ge(S("f2_relu"), n[1])
                o = act32[:, i * 1024:(i + 1) * 1024]
                dve.tensor_tensor(o, gtmp, gtmp, ALU.mult).then_inc(S("f2_act"), 1)

            def square_low(n):
                dve.wait_ge(S("f2_hi"), n)
                dve.tensor_tensor(yL[:], tiles(act32), yH[:].bitcast(F32), ALU.subtract).then_inc(S("f2_lo"), 1)

            def add_down2(g, n, v):
                dve.wait_ge(S("w_used"), v)
                if not isinstance(n, int) or (n - 1) * 4 + g > 0:
                    dve.wait_ge(S("f2_sum"), (n - 1) * 4 + g)
                else:
                    dve.wait_ge(S("o_zero"), 1)
                o = O32[:, 4 * g:4 * g + 4]
                dve.tensor_tensor(o, o, tiles(acc[:, (PHASES["ffn2"][2] + g) % 2]), ALU.add).then_inc(S("f2_sum"), 1)

            def ffn2(n, begin, before, down):
                here = lambda: pl.v + pl.ov
                lo(4 - begin)
                if before:
                    add_down2(3, n - 1, here() - 4)
                if down:
                    square_low(n)
                lo(4)
                lo(4)
                square((0, 2 * n + 1))
                lo(4)
                if down:
                    lo(4)
                square((1, 2 * n + 2))
                if down:
                    for g in range(3):
                        lo(4)
                        add_down2(g, n, here() - 4)

            ffn2(0, 4, False, False)
            ffn2(1, 0, False, True)
            with dve.Fori(0, 6) as i:
                pl.enter(i, 32, 32, 6)
                ffn2(i + 2, 0, True, True)
            pl.leave(6, 32, 32, 6)
            lo(4)
            add_down2(3, 7, pl.v - 4)
            square_low(8)
            for g in range(3):
                lo(4)
                add_down2(g, 8, pl.v - 4)
            add_down2(3, 8, pl.v)
            post_norm(5, 3, "x_done", tiles(blk(4, 2)))


_RAW = ["w_in", "w_proj_a", "w_proj_b", "w_out", "w_ffn_in", "w_ffn_out", "w_ada_2", "w_in_2", "cmp_k_w1_2",
        "cmp_k_w2_2", "cmp_v_w1_2", "cmp_v_w2_2", "w_o_2", "w_up_2", "w_down_2"]


def kernel(**inputs):
    import concourse.bacc as bacc
    from concourse.bass_utils import run_bass_kernel_spmd

    x = {n: np.asarray(a) for n, a in inputs.items()}

    def columns(a):
        return a.reshape(-1, P).T

    consts, lmask = constants()
    arrays = {n: np.ascontiguousarray(x[n][0]) for n in _RAW}
    arrays["xT"] = np.ascontiguousarray(x["x"][0].T)
    arrays["rel_rev"] = np.ascontiguousarray(x["rel_bias"][0][:, ::-1])
    arrays["cols"] = np.ascontiguousarray(np.concatenate(
        [columns(x[n]) for n in ("norm_mix", "norm_ffn", "b_gate", "hgrn_lb_logits", "hgrn_out_gain", "q_gain",
                                 "k_gain", "c_2", "b_ada_2", "pre_norm_mix_2", "post_norm_mix_2", "pre_norm_ffn_2",
                                 "post_norm_ffn_2")] + [x["cmp_k_pos_2"][0].T, x["cmp_v_pos_2"][0].T], axis=1))
    arrays["consts"], arrays["lmask"] = consts, lmask
    nc = bacc.Bacc("TRN2", target_bir_lowering=False, num_devices=1)
    A = {n: nc.dram_tensor(f"in_{n}", a.shape, mybir.dt.from_np(a.dtype), kind="ExternalInput").ap()
         for n, a in arrays.items()}
    out = nc.dram_tensor("out_T", (D, T), F32, kind="ExternalOutput").ap()
    scratch = nc.dram_tensor("bias_ext", (H, EXT), F32, kind="Internal").ap()
    build(nc, A, out, scratch)
    r = run_bass_kernel_spmd(nc, [{f"in_{n}": a for n, a in arrays.items()}], core_ids=[0])
    return np.ascontiguousarray(r.results[0]["out_T"].T)[None]
```

```python
from contextlib import ExitStack

import numpy as np

import concourse.bass as bass
from concourse import mybir

F32 = mybir.dt.float32
F32R = mybir.dt.float32r
U8 = mybir.dt.uint8
ACT = mybir.ActivationFunctionType
ALU = mybir.AluOpType
AX = mybir.AxisListType
ds = bass.ds

P = 128
T = 256
TT = T // P
D = 2048
KT = D // P
H = 8
DA = H * P
N_GATE = 24
CHUNK = 64
N_REL = 191
REL_FUTURE = CHUNK - 1
D_FF1 = 5632
D_FF2 = 8192
CMP_LEN, CMP_STRIDE = 32, 16
N_CMP = (T - CMP_LEN) // CMP_STRIDE + 1
EPS = 1e-6
SCALE = float(P) ** -0.5
MASKED = -1e30
MAX_FLOOR = -1e29
TINY = 1e-30

KU = 2
GCOL = 512
UW = KU * GCOL
NRAW = 4
NSPLIT = 4
GT = GCOL // P
BLK = H * T

COLS = {}
_at = 0
for _name, _n in (("norm_mix", 16), ("norm_ffn", 16), ("b_gate", 32), ("lb", 16), ("out_gain", 8), ("q_gain", 1),
                  ("k_gain", 1), ("c", 16), ("b_ada", 96), ("pre_mix", 16), ("post_mix", 16), ("pre_ffn", 16),
                  ("post_ffn", 16), ("k_pos", 32), ("v_pos", 32)):
    COLS[_name] = _at
    _at += _n
N_COLS = _at

CONST = {}
_at = 0
for _name, _n in (("ident", 128), ("flip", 128), ("swap", 128), ("ones", 128), ("cos", 256), ("sin", 256),
                  ("causal", 256), ("chunk", 256), ("cmp", 256), ("mean", 128),
                  ("head_mean", 1), ("eps", 1)):
    CONST[_name] = _at
    _at += _n
N_CONST = _at
N_LEVEL = 8
EXT = 384


def constants():
    c = np.zeros((P, N_CONST), np.float32)
    i = np.arange(P)
    put = lambda name, a: c.__setitem__((slice(None), slice(CONST[name], CONST[name] + a.shape[1])), a)
    put("ident", np.eye(P, dtype=np.float32))
    put("flip", np.eye(P, dtype=np.float32)[::-1])
    put("swap", np.roll(np.eye(P, dtype=np.float32), P // 2, axis=0))
    put("ones", np.ones((P, P), np.float32))
    inv = np.float32(10000.0) ** (-np.arange(0, P, 2, dtype=np.float32) / np.float32(P))
    ang = (np.arange(T, dtype=np.float32)[:, None] * inv[None, :]).astype(np.float32).T
    put("cos", np.concatenate([np.cos(ang), np.cos(ang)]).astype(np.float32))
    put("sin", np.concatenate([-np.sin(ang), np.sin(ang)]).astype(np.float32))
    tri = np.where(i[None, :] > i[:, None], np.float32(MASKED), np.float32(0))
    put("causal", np.concatenate([np.zeros((P, P), np.float32), tri], 1))
    ch = np.where(i[None, :] // CHUNK > i[:, None] // CHUNK, np.float32(MASKED), np.float32(0))
    put("chunk", np.concatenate([np.zeros((P, P), np.float32), ch], 1))
    end = i * CMP_STRIDE + CMP_LEN - 1
    cm = [np.where((i[None, :] < N_CMP) & (end[None, :] <= t0 + i[:, None]), np.float32(0), np.float32(MASKED))
          for t0 in (0, P)]
    put("cmp", np.concatenate(cm, 1))
    put("eps", np.full((P, 1), EPS, np.float32))
    put("mean", np.full((P, P), 1.0 / D, np.float32))
    put("head_mean", np.full((P, 1), 1.0 / P, np.float32))
    m = np.zeros((P, N_LEVEL, P), np.float32)
    m[:, 0] = np.eye(P, dtype=np.float32)
    s, t = i[:, None], i[None, :]
    for lev in range(1, N_LEVEL):
        b = 1 << (lev - 1)
        m[:, lev] = (s // (2 * b) == t // (2 * b)) & (s % (2 * b) < b) & (t % (2 * b) >= b)
    return c, m.reshape(P, N_LEVEL * P)


PHASES = {}


def plan():
    v = g = 0
    for name, groups, units in (
            ("f", 2, 8), ("q", 2, 8), ("i", 2, 8), ("g", 2, 8), ("qb", 2, 8), ("kb", 2, 8), ("vb", 2, 8),
            ("gate_a", 4, 8), ("proj_a", 4, 4), ("gate_b", 4, 8), ("proj_b", 4, 4), ("out", 4, 8), ("ffn1", 66, 4),
            ("cmp_kv", 1, 8), ("qn", 2, 8), ("selwin", 2, 8), ("moba", 6, 8), ("wo", 8, 4), ("ffn2", 48, 4)):
        PHASES[name] = (v, g)
        v += groups * units
        if name == "selwin":
            v += 8
        g += groups


plan()

HALF = range(1, 64, 2)
THIRD = range(2, 24, 3)
EIGHTH = range(3, 64, 8)
ADA = {"q_i": [p for p in HALF if p < 32], "out": [p for p in HALF if p < 32],
       "ffn1_first": [p for p in HALF if p < 16], "ffn1": THIRD,
       "qn": [p for p in HALF if p < 16], "moba": [p for p in HALF if p < 48], "wo": [p for p in HALF if p < 16],
       "ffn2_first": range(1, 16, 4), "ffn2": [p for p in EIGHTH if p < 32]}


class Place:

    def __init__(self):
        self.u = self.v = self.g = self.a = self.j = 0
        self.ou = self.ov = self.og = self.oa = 0
        self.at, self.ada, self.looping = 0, (), False

    def phase(self, name):
        self.at, self.ada = 0, ADA[name]

    def follows(self):
        self.at += 1
        return self.at - 1 in self.ada

    def past(self):
        self.u += 1
        self.j = (self.j + 1) % 8
        self.a += self.j == 0
        return self.j == 0

    def enter(self, i, u, v, g, a=0):
        self.ou, self.ov, self.og, self.oa, self.looping = i * u, i * v, i * g, i * a, True

    def leave(self, n, u, v, g, a=0):
        self.ou = self.ov = self.og = self.oa = 0
        self.looping = False
        self.u += (n - 1) * u
        self.v += (n - 1) * v
        self.g += (n - 1) * g
        self.a += (n - 1) * a


def build(nc, A, out, scratch):
    with ExitStack() as ctx:
        def sb(name, shape, dt=F32):
            return ctx.enter_context(nc.sbuf_tensor(name, shape, dt))

        sems = {}

        def S(name):
            if name not in sems:
                sems[name] = ctx.enter_context(nc.semaphore(name))
            return sems[name]

        raw = sb("raw", [P, NRAW, UW])
        whi = sb("whi", [P, NSPLIT, UW], F32R)
        wlo = sb("wlo", [P, NSPLIT, UW], F32R)
        hH = sb("hH", [P, KT, T], F32R)
        hL = sb("hL", [P, KT, T], F32R)
        yH = sb("yH", [P, H, T], F32R)
        yL = sb("yL", [P, H, T], F32R)
        arena = sb("arena", [P, 11 * BLK + BLK // 2])
        cst = sb("cst", [P, N_CONST])
        col = sb("col", [P, N_COLS])
        lmask = sb("lmask", [P, N_LEVEL * P], U8)
        rstd = sb("rstd", [P, T])
        q_scale = sb("q_scale", [P, 1])
        lb = sb("lb", [P, 6, H])
        unused = sb("unused", [P, 1])
        rr = sb("rr", [P, 2, 2 * H])
        cs = sb("cs", [P, KT])
        adaacc = sb("adaacc", [P, 2, GCOL])
        mod = sb("mod", [P, 96])
        modA = sb("modA", [P, 4, KT])
        stat = sb("stat", [P, 4, 3, 2])
        gates = sb("gates", [P, TT, N_GATE])
        wgh = sb("wgh", [P, KT, N_GATE], F32R)
        wgl = sb("wgl", [P, KT, N_GATE], F32R)

        acc = ctx.enter_context(nc.psum_tensor("acc", [P, 2, 2 * GCOL], F32))
        W = ctx.enter_context(nc.psum_tensor("W", [P, 4, 512], F32))
        Wf = W[:].rearrange("p a b -> p (a b)")

        def blk(i, n=1):
            return arena[:, i * BLK:int((i + n) * BLK)]

        def tiles(ap, t=T):
            return ap.rearrange("p (k t) -> p k t", t=t)

        def C(name, n=P):
            return cst[:, CONST[name]:CONST[name] + n]

        def V(name, n=1, at=0):
            return col[:, COLS[name] + at:COLS[name] + at + n]

        ident, ones, flip, swap = C("ident"), C("ones"), C("flip"), C("swap")
        one = C("ones", 1)
        epsc = C("eps", 1)
        x0 = tiles(blk(0, 2))
        sq0 = tiles(blk(2, 2))
        qa, ka, ia, ga = blk(0), blk(1), blk(2), blk(3)
        qb, kb, vb = blk(4), blk(5), blk(6)
        bc, Cb, ST, ob = blk(7), blk(8), blk(9), blk(10)
        off = blk(11, 0.5)
        iav = ia.rearrange("p (t n) -> p t n", t=TT)
        vbv = vb.rearrange("p (t n) -> p t n", t=TT)
        lmaskf = blk(4, 0.5)
        M = blk(0, 2)
        HK = blk(3)
        yb = blk(7)
        sgb = blk(8, 2)
        sb3 = blk(10)[:, 0:3 * 384].rearrange("p (r n) -> p r n", r=3)
        pt2 = blk(11, 0.5)[:, 0:2 * 384].rearrange("p (r n) -> p r n", r=2)
        X = tiles(blk(2, 2))
        gtmp = blk(4, 0.5)
        act32 = blk(5)
        O32 = tiles(blk(0, 2))
        kvc = tiles(blk(0, 0.5))
        ksel, kwin = tiles(arena[:, 1024:1536]), tiles(arena[:, 1536:2048])
        vsel = arena[:, 2048:2560].rearrange("p (t n) -> p t n", t=TT)
        vwin = arena[:, 2560:3072].rearrange("p (t n) -> p t n", t=TT)
        cx = blk(9)
        cxp = [y[:].rearrange("p a b -> p (a b)")[:, 0:60 * CMP_LEN].rearrange("p (l e c) -> p l e c", e=2, c=30)
               for y in (yH, yL)]
        hidP = W[:, 3, 0:128].rearrange("p (k c) -> p k c", k=2)
        hid = arena[:, 3072:3584].rearrange("p (k g c) -> p k g c", k=2, g=2)
        kcT = arena[:, 3584:3840].rearrange("p (g c) -> p g c", g=2)
        vcm = arena[:, 3840:4096].rearrange("p (g d) -> p g d", g=2)
        qn, qm, km, vm, on, om = blk(4), blk(5), blk(6), blk(7), blk(8), blk(9)
        vmv = vm.rearrange("p (t n) -> p t n", t=TT)
        hsg = blk(9)[:, 960:1020].rearrange("p (k c) -> p k c", k=2)
        hsum = blk(9)[:, 1984:2044].rearrange("p (k c) -> p k c", k=2)
        rope = blk(10)[:, 3 * 384:3 * 384 + GCOL]
        wg = blk(7)[:, 0:KT * N_GATE].rearrange("p (k n) -> p k n", k=KT)
        w2 = blk(7)[:, 384:384 + 2 * P].rearrange("p (k n) -> p k n", k=2)
        gateT = arena[0:N_GATE, 11 * BLK + 768:11 * BLK + 768 + T]
        ext = arena[0:H, 10 * BLK:10 * BLK + EXT]
        modP = W[:, 2, 384:480]

        wv = {n: A[n].rearrange("(k p) n -> p k n", p=P) for n in
              ("w_in", "w_proj_a", "w_proj_b", "w_out", "w_ffn_in", "w_ffn_out", "w_ada_2", "w_in_2", "w_o_2",
               "w_up_2", "w_down_2", "cmp_k_w1_2", "cmp_v_w1_2")}
        landed = [S(f"landed{i}") for i in range(NRAW)]

        jobs = []
        for h in range(H):
            hd = slice(h * T, (h + 1) * T)
            jobs.append(("bias", qb[:, hd], kb[:, hd], [vbv[:, t, h * P:(h + 1) * P] for t in range(TT)],
                         yb[:, hd], h, True, True, None))
        N_B = len(jobs)
        for h in range(H):
            hd, g = slice(h * T, (h + 1) * T), h // 4
            gt = [gates[:, t, 3 * h:3 * h + 3] for t in range(TT)]
            jobs.append(("causal", qn[:, hd], ksel[:, g], [vsel[:, t, g * P:(g + 1) * P] for t in range(TT)],
                         on[:, hd], H + h, True, False, [x[:, 1:2] for x in gt]))
            jobs.append(("causal", qn[:, hd], kwin[:, g], [vwin[:, t, g * P:(g + 1) * P] for t in range(TT)],
                         on[:, hd], H + h, False, False, [x[:, 2:3] for x in gt]))
            jobs.append(("cmp", qn[:, hd], kcT[:, g], [vcm[:, g]], on[:, hd], H + h, False, True,
                         [x[:, 0:1] for x in gt]))
        N_N = len(jobs)
        for h in range(H):
            hd = slice(h * T, (h + 1) * T)
            jobs.append(("causal", qm[:, hd], km[:, hd], [vmv[:, t, h * P:(h + 1) * P] for t in range(TT)],
                         om[:, hd], 2 * H + h, True, True, None))
        N_M = len(jobs)
        last_of = {j[5]: n for n, j in enumerate(jobs) if j[7]}

        def parts(kind):
            return [(0, P), (P, 2 * P if kind == "cmp" else 3 * P)]

        def mask_of(kind, t):
            if kind == "cmp":
                return cst[:, CONST["cmp"] + t * P:CONST["cmp"] + (t + 1) * P]
            at = CONST["chunk" if kind == "bias" else "causal"]
            return cst[:, at + P:at + 2 * P] if t == 0 else cst[:, at:at + 2 * P]

        block = ctx.enter_context(nc.Block())

        @block.sync
        def _(sp):
            pl = Place()

            def load(src, shape=None, split=True):
                s = pl.u % NRAW
                if pl.u >= NRAW:
                    sp.wait_ge(S("unit_done"), pl.u + pl.ou - NRAW + 1)
                dst = raw[:, s].rearrange("p (k n) -> p k n", k=shape or KU)
                sp.dma_start(dst, src).then_inc(landed[s], 16)
                pl.u += 1
                if split and pl.follows():
                    c0 = (pl.a + pl.oa) * GCOL
                    c = ds(c0, GCOL) if pl.looping else slice(c0, c0 + GCOL)
                    load(wv["w_ada_2"][:, pl.j * KU:(pl.j + 1) * KU, c], split=False)
                    pl.u -= 1
                    pl.past()

            def group(w, c0, units, k0=0):
                for u in range(units):
                    load(wv[w][:, k0 + u * KU:k0 + (u + 1) * KU, c0:c0 + GCOL])

            def looped(w, c0, groups, units, k0=0):
                with sp.Fori(0, groups) as i:
                    pl.enter(i, units, 0, 0)
                    for u in range(units):
                        load(wv[w][:, k0 + u * KU:k0 + (u + 1) * KU, ds(i * GCOL + c0, GCOL)])
                pl.leave(groups, units, 0, 0)

            for c in range(4):
                src = A["xT"].rearrange("(k p) t -> p k t", p=P)[:, 4 * c:4 * c + 4]
                sp.dma_start(x0[:, 4 * c:4 * c + 4], src).then_inc(S(f"x_in{c}"), 16)
            sp.dma_start(cst[:], A["consts"]).then_inc(S("tables_in"), 16)
            sp.dma_start(col[:], A["cols"]).then_inc(S("tables_in"), 16)
            group("w_in", DA, 8)
            group("w_in", DA + GCOL, 8)
            pl.phase("q_i")
            with sp.Fori(0, 2) as i:
                pl.enter(i, 24, 0, 0, 1)
                for j in range(2):
                    for u in range(8):
                        load(wv["w_in"][:, u * KU:(u + 1) * KU, ds(i * 2 * DA + j * GCOL, GCOL)])
            pl.leave(2, 24, 0, 0, 1)
            pl.ada = ()
            looped("w_in", 3 * DA, 12, 8)
            looped("w_proj_a", 0, 4, 4)
            looped("w_in", 7 * DA + D, 4, 8)
            looped("w_proj_b", 0, 4, 4)
            pl.phase("out")
            with sp.Fori(0, 2) as i:
                pl.enter(i, 24, 0, 0, 1)
                for j in range(2):
                    for u in range(8):
                        load(wv["w_out"][:, u * KU:(u + 1) * KU, ds(i * 2 * GCOL + j * GCOL, GCOL)])
            pl.leave(2, 24, 0, 0, 1)

            def ffn1(i, down):
                pl.phase("ffn1" if down else "ffn1_first")
                for half in range(2):
                    for u in range(8):
                        load(wv["w_ffn_in"][:, u * KU:(u + 1) * KU, ds(i * GCOL + half * D_FF1, GCOL)])
                if down:
                    for g in range(4):
                        for u in range(2):
                            load(wv["w_ffn_out"][:, ds(i * GT + (u * KU - GT), KU), g * GCOL:(g + 1) * GCOL])

            ffn1(0, False)
            with sp.Fori(0, 10) as i:
                pl.enter(i, 32, 0, 0, 1)
                ffn1(i + 1, True)
            pl.leave(10, 32, 0, 0, 1)
            for g in range(4):
                group_k = D_FF1 // P - GT
                for u in range(2):
                    load(wv["w_ffn_out"][:, group_k + u * KU:group_k + (u + 1) * KU, g * GCOL:(g + 1) * GCOL])

            group("w_in_2", DA, 8)
            pl.phase("qn")
            group("w_in_2", 0, 8)
            group("w_in_2", GCOL, 8)
            for u in range(8):
                load(wv["w_in_2"][:, u * KU:(u + 1) * KU, DA + GCOL:DA + 2 * GCOL])
                w = wv["cmp_v_w1_2" if u // 4 else "cmp_k_w1_2"]
                load(w[:, (u % 4) * 8:(u % 4 + 1) * 8, :], shape=8)
            group("w_in_2", DA + 2 * GCOL, 8)
            pl.phase("moba")
            with sp.Fori(0, 3) as i:
                pl.enter(i, 24, 0, 0, 1)
                for j in range(2):
                    for u in range(8):
                        c0 = DA + 3 * GCOL + N_GATE + j * GCOL
                        load(wv["w_in_2"][:, u * KU:(u + 1) * KU, ds(i * 2 * GCOL + c0, GCOL)])
            pl.leave(3, 24, 0, 0, 1)
            pl.ada = ()
            looped("w_o_2", 0, 4, 4)
            pl.phase("wo")
            for g in range(4):
                group("w_o_2", g * GCOL, 4, k0=8)

            def up(i):
                for j in range(2):
                    for u in range(8):
                        load(wv["w_up_2"][:, u * KU:(u + 1) * KU, ds(i * 2 * GCOL + j * GCOL, GCOL)])

            def down(i):
                for g in range(4):
                    for u in range(4):
                        load(wv["w_down_2"][:, ds(i * 8 + u * KU, KU), g * GCOL:(g + 1) * GCOL])

            pl.phase("ffn2_first")
            up(0)
            pl.phase("ffn2")
            up(1)
            down(0)
            with sp.Fori(0, 3) as i:
                pl.enter(i, 72, 0, 0, 1)
                for r in range(2):
                    pl.phase("ffn2")
                    up(i * 2 + (r + 2))
                    down(i * 2 + (r + 1))
            pl.leave(3, 72, 0, 0, 1)
            down(7)
            for c in range(4):
                sp.wait_ge(S("x_done"), c + 1)
                q = slice(4 * c, 4 * c + 4)
                sp.dma_start(out.rearrange("(k p) t -> p k t", p=P)[:, q], X[:, q]).then_inc(S("stored"), 16)
            sp.wait_ge(S("stored"), 64)

        @block.gpsimd
        def _(pool):
            pool.dma_start(lmaskf, A["lmask"]).then_inc(S("mask_in"), 16)
            pool.memset(ST, 0.0).then_inc(S("st_zero"), 1)
            pool.dma_start(ext[:, P:P + N_REL], A["rel_rev"]).then_inc(S("ext_in"), 16)
            pool.wait_ge(S("ext_full"), 2)
            pool.dma_start(scratch, ext).then_inc(S("ext_out"), 16)
            pool.wait_ge(S("ext_out"), 16)
            pool.wait_ge(S("hn_done"), 1)
            src = bass.AP(scratch.tensor, 0, [[1, P], [EXT, H], [1, T]])
            pool.dma_start(tiles(HK), src).then_inc(S("hk_in"), 16)
            pool.wait_ge(S("att_s"), N_B)
            pool.dma_start(X, A["xT"].rearrange("(k p) t -> p k t", p=P)).then_inc(S("x_again"), 16)
            pool.wait_ge(S("merged"), 4)
            pool.dma_start(wg, wv["w_in_2"][:, :, DA + 3 * GCOL:DA + 3 * GCOL + N_GATE]).then_inc(S("wg_in"), 16)
            pool.dma_start(w2[:, 0], A["cmp_k_w2_2"]).then_inc(S("wg_in"), 16)
            pool.dma_start(w2[:, 1], A["cmp_v_w2_2"]).then_inc(S("wg_in"), 16)
            pool.wait_ge(S("h_lo"), 12)
            pool.memset(hid.rearrange("p k g c -> p (k g c)"), 0.0).then_inc(S("hid_zero"), 1)
            pool.wait_ge(S("h_lo"), 16)
            pool.memset(blk(0, 2), 0.0).then_inc(S("o_zero"), 1)

        @block.scalar
        def _(act):
            pl = Place()

            def hi():
                s, v = pl.u % NRAW, pl.v % NSPLIT
                act.wait_ge(landed[s], 16 * (pl.u // NRAW + 1) + pl.ou * (16 // NRAW))
                if pl.v >= NSPLIT:
                    act.wait_ge(S("w_used"), pl.v + pl.ov - NSPLIT + 1)
                act.activation(whi[:, v], raw[:, s], ACT.Copy).then_inc(S("w_hi"), 1)
                pl.u += 1
                pl.v += 1
                if pl.follows():
                    pl.past()

            def group(units=8, hooks={}, begin=0):
                for u in range(begin, units):
                    hi()
                    if u in hooks:
                        hooks[u]()
                pl.g += 1

            def full(g, v):
                act.wait_ge(S("w_used"), v)
                return acc[:, g % 2]

            def square(k, c, src, sq):
                q = slice(4 * c, 4 * c + 4)
                act.activation(sq[:, q], src[:, q], ACT.Square).then_inc(S("nm_sq"), 1)

            def root_table():
                act.activation(unused[:], epsc, ACT.Sqrt)

            def root(k):
                act.wait_ge(S("nm_sum"), k + 1)
                act.activation(rstd[:], W[:, 3, 0:T], ACT.Sqrt, bias=epsc).then_inc(S("nm_root"), 1)

            def norm_hi(k, c, h32, shift=None):
                act.wait_ge(S("h_ready"), 4 * k + c + 1)
                if shift is None:
                    ins = act.activation(hH[:, 4 * c:4 * c + 4], h32[:, 4 * c:4 * c + 4], ACT.Copy)
                else:
                    for j in range(4 * c, 4 * c + 4):
                        ins = act.activation(hH[:, j], h32[:, j], ACT.Identity, bias=mod[:, shift + j:shift + j + 1])
                ins.then_inc(S("h_hi"), 1)

            for c in range(4):
                act.wait_ge(S(f"x_in{c}"), 16)
                square(0, c, x0, sq0)
            act.wait_ge(S("tables_in"), 32)
            root_table()
            root(0)
            for c in range(4):
                norm_hi(0, c, sq0)
                hi()
            act.wait_ge(S("lb_step"), 1)
            act.activation(lb[:, 0:2], lb[:, 0:2], ACT.Exp).then_inc(S("lb_exp"), 1)
            act.activation(cs[:], V("c", 16), ACT.Sigmoid).then_inc(S("c_sig"), 1)

            def evac_sig(g, v, dst, sem):
                def run():
                    a = full(g, v)
                    ins = act.activation(dst, a, ACT.Sigmoid)
                    ins.then_inc(S(sem), 1)
                return run

            def evac_copy(g, v, dst, sem, tokens=False):
                def run():
                    a = full(g, v)
                    if tokens:
                        a = a.rearrange("p (t n) -> p t n", t=TT)
                    act.activation(dst, a, ACT.Copy).then_inc(S(sem), 1)
                return run

            def half(b, i):
                return b[:, i * 1024:(i + 1) * 1024]

            def halfv(b, i):
                return b[:, :, i * GCOL:(i + 1) * GCOL]

            def level_exp(l):
                def run():
                    act.wait_ge(S("c_diff"), l)
                    if l < 8:
                        b = 1 << (l - 1)
                        v = Cb.rearrange("p (n h b) -> p n h b", h=2, b=b)
                        act.activation(v[:, :, 0], v[:, :, 0], ACT.Exp, scale=-1.0)
                        act.activation(v[:, :, 1], v[:, :, 1], ACT.Exp).then_inc(S("c_exp"), 1)
                    else:
                        v = Cb.rearrange("p (h t s) -> p h t s", h=H, t=TT)
                        bv = bc.rearrange("p (h t s) -> p h t s", h=H, t=TT)
                        act.activation(v[:, :, 0], v[:, :, 0], ACT.Exp, scale=-1.0)
                        act.activation(v[:, :, 1], bv[:, :, 1], ACT.Exp).then_inc(S("c_exp"), 1)
                return run

            group(begin=4)
            group(hooks={3: evac_sig(0, 8, half(ka, 0), "sig_f")})
            pl.phase("q_i")
            group(hooks={3: evac_sig(1, 16, half(ka, 1), "sig_f")})
            def sig_q(g, v, i):
                return evac_sig(g, v, half(qa, i), "sig_q")
            group(hooks={3: sig_q(2, 24, 0)})

            def ln_f():
                act.wait_ge(S("f_in"), 2)
                act.activation(Cb, Cb, ACT.Ln).then_inc(S("ln_f"), 1)
            group(hooks={3: sig_q(3, 32, 1), 5: ln_f})
            group(hooks={3: evac_copy(4, 40, halfv(iav, 0), "i_in", True)})
            group(hooks={3: evac_copy(5, 48, halfv(iav, 1), "i_in", True)})
            group(hooks={3: evac_sig(6, 56, half(ga, 0), "sig_g"), 6: level_exp(1)})
            group(hooks={3: evac_sig(7, 64, half(ga, 1), "sig_g"), 6: level_exp(2)})
            group(hooks={3: evac_copy(8, 72, half(qb, 0), "qk_in"), 6: level_exp(3)})
            group(hooks={3: evac_copy(9, 80, half(qb, 1), "qk_in"), 6: level_exp(4)})
            group(hooks={3: evac_copy(10, 88, half(kb, 0), "qk_in"), 6: level_exp(5)})
            group(hooks={3: evac_copy(11, 96, half(kb, 1), "qk_in"), 6: level_exp(6)})
            group(hooks={3: evac_copy(12, 104, halfv(vbv, 0), "vb_in", True), 6: level_exp(7)})

            def off_copy():
                act.wait_ge(S("lvl"), 9)
                act.activation(off, Wf[:, 0:H * P], ACT.Copy).then_inc(S("off_in"), 1)

            def head_square(k):
                def run():
                    src = (ob, qb, kb)[k]
                    if k == 0:
                        act.wait_ge(S("o_mm"), 1)
                        act.wait_ge(S("ext_out"), 16)
                        act.activation(ob, Wf, ACT.Copy).then_inc(S("o_in"), 1)
                        act.wait_ge(S("o_in"), 1)
                    else:
                        act.wait_ge(S("hn_sum"), k)
                        act.wait_ge(S("qk_in"), 4)
                    act.activation(Cb, src, ACT.Square).then_inc(S("hn_sq"), 1)
                return run

            def head_root(k):
                def run():
                    act.wait_ge(S("hn_sum"), k + 1)
                    act.activation(rr[:, 0], W[:, 3, 0:2 * H], ACT.Sqrt, bias=epsc)\
                       .then_inc(S("hn_root"), 1)
                return run

            def ya_hi():
                act.wait_ge(S("hn_done"), 1)
                act.activation(yH[:], tiles(ob), ACT.Copy).then_inc(S("y_hi"), 1)

            def gate_sig(g, v, dst, at):
                def run():
                    a = full(g, v)
                    for m in range(GT):
                        ins = act.activation(dst[:, m * T:(m + 1) * T], a[:, m * T:(m + 1) * T], ACT.Sigmoid,
                                             bias=V("b_gate", 1, at + m))
                    ins.then_inc(S("gate_in"), 1)
                return run

            group(hooks={3: evac_copy(13, 112, halfv(vbv, 1), "vb_in", True), 6: level_exp(8)})

            def mg(i):
                return M[:, i * 1024:(i + 1) * 1024]

            def first_gate():
                act.wait_ge(S("c_done"), 8)
                gate_sig(14, 120, mg(0), 0)()
            group(hooks={2: off_copy, 3: first_gate, 5: head_square(0)})
            group(hooks={0: head_root(0), 1: head_square(1), 3: gate_sig(15, 128, mg(1), 4),
                         4: ya_hi, 5: head_root(1), 6: head_square(2)})
            group(hooks={2: head_root(2), 3: gate_sig(16, 136, mg(2), 8)})

            def att(n, n0, n1):
                if n0 <= n - 3 < n1 and jobs[n - 3][7]:
                    kind, q, k, vs, y, head, fst, lst, gt = jobs[n - 3]
                    act.wait_ge(S("att_pv"), n - 3 + 1)
                    act.activation(y, W[:, 3, (head % 2) * T:(head % 2 + 1) * T], ACT.Copy)\
                       .then_inc(S("att_y"), 1)
                if n0 <= n - 2 < n1:
                    m = n - 2
                    width = parts(jobs[m][0])[1][1]
                    act.wait_ge(S("att_t"), m + 1)
                    if m >= 2:
                        act.wait_ge(S("att_pv"), m - 1)
                    act.activation(pt2[:, m % 2, 0:width], W[:, 2, 0:width], ACT.Copy).then_inc(S("att_pt"), 1)
                if n0 <= n < n1:
                    kind = jobs[n][0]
                    act.wait_ge(S("att_neg"), n + 1)
                    for t, (a, b) in enumerate(parts(kind)):
                        p = sb3[:, n % 3, a:b]
                        ins = act.activation(p, p, ACT.Exp, bias=stat[:, 1, n % 3, t:t + 1],
                                             scale=1.0 if kind == "bias" else SCALE,
                                             accum_out=stat[:, 2, n % 3, t:t + 1])
                    ins.then_inc(S("att_exp"), 1)

            def slot(n, n0, n1):
                return lambda: att(n, n0, n1)

            g0, v0 = PHASES["proj_a"][1], PHASES["proj_a"][0]
            group(4, hooks={2: slot(0, 0, N_B), 3: gate_sig(17, 144, mg(3), 12)})
            for i in range(1, 4):
                group(4, hooks={2: slot(i, 0, N_B)})
            sg = lambda i: sgb[:, i * 1024:(i + 1) * 1024]
            def yb_hi():
                act.wait_ge(S("w_used"), PHASES["gate_b"][0])
                act.wait_ge(S("att_y"), H)
                act.activation(yH[:], tiles(yb), ACT.Copy).then_inc(S("y_hi"), 1)
            for i in range(4):
                hooks = {2: slot(4 + 2 * i, 0, N_B), 6: slot(5 + 2 * i, 0, N_B)}
                if i == 3:
                    hooks[6] = yb_hi
                if i:
                    hooks[3] = gate_sig(22 + i - 1, PHASES["gate_b"][0] + 8 * i, sg(i - 1), 16 + 4 * (i - 1))
                group(hooks=hooks)

            def merged_hi(c):
                act.wait_ge(S("w_used"), PHASES["proj_b"][0])
                act.wait_ge(S("merged"), c + 1)
                act.activation(hH[:, 4 * c:4 * c + 4], tiles(M)[:, 4 * c:4 * c + 4], ACT.Copy).then_inc(S("m_hi"), 1)
            for _ in range(4):
                hi()
            gate_sig(25, PHASES["gate_b"][0] + 32, sg(3), 28)()
            pl.g += 1
            group(4)
            for i in range(2, 4):
                group(4, hooks={1: lambda: merged_hi(i - 2)})
            pl.phase("out")
            hi()
            hi()
            merged_hi(2)
            hi()
            hi()
            merged_hi(3)
            for _ in range(4):
                hi()
            pl.g += 1

            def square_x1(c):
                def run():
                    act.wait_ge(S("x1"), c + 1)
                    if c == 0:
                        act.wait_ge(S("m_lo"), 4)
                    square(1, c, X, tiles(M))
                return run
            for i in range(1, 4):
                group(hooks={4: square_x1(i - 1)})
            pl.phase("ffn1_first")
            for _ in range(4):
                hi()
            root_table()
            square_x1(3)()
            root(1)
            for c in range(4):
                norm_hi(1, c, tiles(M))

            G1 = PHASES["ffn1"][1]

            def ffn_sig(g, vpos):
                act.wait_ge(S("w_used"), vpos)
                act.activation(gtmp, acc[:, g % 2], ACT.Sigmoid).then_inc(S("ff_sig"), 1)

            def ffn1(begin, down, n):
                if down:
                    pl.phase("ffn1")
                    hi(); hi(); hi(); hi()
                    act.wait_ge(S("ff_act"), n)
                    act.wait_ge(S("w_used"), pl.v + pl.ov - 4)
                    act.activation(yH[:, 0:GT], tiles(act32[:, 0:1024]), ACT.Copy).then_inc(S("ff_hi"), 1)
                    hi(); hi(); hi(); hi()
                else:
                    for _ in range(begin, 8):
                        hi()
                for _ in range(4):
                    hi()
                ffn_sig(pl.g, pl.v + pl.ov - 4)
                for _ in range(4):
                    hi()
                if down:
                    for _ in range(8):
                        hi()
                pl.g += 6 if down else 2

            ffn1(4, False, 0)
            with act.Fori(0, 10) as i:
                pl.enter(i, 32, 24, 6, 1)
                ffn1(0, True, i + 1)
            pl.leave(10, 32, 24, 6, 1)
            for _ in range(4):
                hi()
            act.wait_ge(S("ff_act"), 11)
            act.activation(yH[:, GT:], tiles(act32[:, 0:1024]), ACT.Copy).then_inc(S("ff_hi"), 1)
            for _ in range(4):
                hi()
            pl.g += 4
            for c, ahead in enumerate((0, 2, 2, 0)):
                for _ in range(ahead):
                    hi()
                if c == 3:
                    root_table()
                act.wait_ge(S("ff_sum"), 40 + c + 1)
                square(2, c, X, O32)
            root(2)
            for c in range(4):
                norm_hi(2, c, O32, 0)
            act.wait_ge(S("wg_in"), 48)
            act.activation(wgh[:], wg[:], ACT.Copy).then_inc(S("wg_hi"), 1)

            def rope_raw(n, g, v, c0, width, vdst=None):
                def run():
                    act.wait_ge(S("w_used"), v)
                    if vdst is not None:
                        act.activation(vdst, acc[:, g % 2, GCOL:].rearrange("p (t n) -> p t n", t=TT), ACT.Copy)\
                           .then_inc(S("kv_in"), 1)
                    if n >= 1:
                        act.wait_ge(S("roped"), n)
                    act.activation(rope[:, 0:width], acc[:, g % 2, c0:c0 + width], ACT.Copy).then_inc(S("rope_raw"), 1)
                return run

            v2, gg = PHASES["cmp_kv"][0], PHASES["cmp_kv"][1]
            group(begin=4)
            pl.phase("qn")
            group(hooks={3: rope_raw(0, gg, v2 + 8, 0, GCOL, kvc[:, 2:4])})

            def x_hi(kind):
                def run():
                    act.wait_ge(S("cx"), kind + 1)
                    src = cx[:, kind * 1024:kind * 1024 + 960].rearrange("p (l c) -> p l c", c=30)
                    act.activation(cxp[kind][:, :, 0], src, ACT.Copy).then_inc(S("cx_hi"), 1)
                return run
            group(hooks={3: rope_raw(1, gg + 1, v2 + 16, 0, GCOL), 4: x_hi(0), 5: x_hi(1),
                         7: rope_raw(2, gg + 1, v2 + 16, GCOL, GCOL)})
            def also(*fs):
                return lambda: [f() for f in fs]

            def hid_sig():
                act.wait_ge(S("hid_sum"), 1)
                act.activation(hsg, hsum, ACT.Sigmoid).then_inc(S("hid_sig"), 1)

            def gates_sig():
                act.wait_ge(S("gates_mm"), 1)
                act.activation(gateT, W[0:N_GATE, 2, 0:T], ACT.Sigmoid).then_inc(S("gates_sig"), 1)

            def gates_copy():
                act.wait_ge(S("gates_turn"), 1)
                act.activation(gates[:].rearrange("p t n -> p (t n)"), W[:, 2, 0:TT * N_GATE], ACT.Copy)\
                   .then_inc(S("gates_in"), 1)

            def kvc_copy():
                act.wait_ge(S("cmp_kv"), 1)
                act.activation(kcT.rearrange("p g c -> p (g c)"), W[:, 0, 0:2 * P], ACT.Copy)
                act.activation(vcm.rearrange("p g c -> p (g c)"), W[:, 0, 2 * P:4 * P], ACT.Copy)\
                   .then_inc(S("kvc_in"), 1)
            for u in range(8):
                hi()
                hi()
                if u == 1:
                    rope_raw(3, gg + 2, v2 + 24, 0, GCOL)()
                if u == 4:
                    rope_raw(4, gg + 2, v2 + 24, GCOL, GCOL)()
                if u == 3:
                    gates_sig()
                if u == 7:
                    gates_copy()
            pl.g += 1
            group(hooks={3: rope_raw(5, gg + 3, v2 + 39, 0, GCOL, vsel), 4: hid_sig, 7: kvc_copy})
            pl.phase("moba")
            n = N_B
            for j in range(6):
                hooks = {}
                for u in ((4, 7) if j == 0 else (0, 2, 4, 6)):
                    hooks[u] = slot(n, N_B, N_N)
                    n += 1
                end = v2 + 48 + 8 * j
                if j == 0:
                    hooks[3] = rope_raw(6, gg + 4, end, 0, GCOL, vwin)
                elif j <= 4:
                    r = 7 + 2 * (j - 1)
                    hooks[3] = rope_raw(r, gg + 4 + j, end, 0, GCOL)
                    hooks[7] = rope_raw(r + 1, gg + 4 + j, end, GCOL, GCOL)
                else:
                    hooks[3] = evac_copy(gg + 9, end, halfv(vmv, 0), "vm_in", True)
                group(hooks=hooks)
            for u in range(4):
                hi()
                att(n, N_B, N_N)
                n += 1
            evac_copy(gg + 10, v2 + 96, halfv(vmv, 1), "vm_in", True)()
            att(n, N_B, N_N)
            assert n == N_N + 2
            act.wait_ge(S("att_y"), 2 * H)
            act.activation(yH[:], tiles(on), ACT.Copy).then_inc(S("y_hi"), 1)
            pl.g += 1
            n = N_N
            gw, vw = PHASES["wo"][1], PHASES["wo"][0]

            def wo_copy(i):
                return evac_copy(gw + i, vw + 4 * (i + 1), blk(0, 2)[:, i * 1024:(i + 1) * 1024], "wo_in")
            for i in range(1, 4):
                group(4, hooks={1: slot(n, N_N, N_M), 2: slot(n + 1, N_N, N_M),
                                3: also(wo_copy(i - 1), slot(n + 2, N_N, N_M))})
                n += 3
            pl.phase("wo")
            hi()
            hi()
            att(n, N_N, N_M)
            hi()
            hi()
            wo_copy(3)()
            att(n + 1, N_N, N_M)
            assert n + 1 == N_M + 2
            act.wait_ge(S("att_y"), 3 * H)
            act.activation(hH[:, 0:8], tiles(om), ACT.Copy).then_inc(S("om_hi"), 1)
            pl.g += 1
            def square_o(c):
                def run():
                    act.wait_ge(S("o_sum"), c + 1)
                    square(3, c, O32, tiles(blk(4, 2)))
                return run
            group(4)
            for i in range(2, 4):
                group(4, hooks={1: square_o(i - 2)})
            pl.phase("ffn2_first")
            hi()
            hi()
            square_o(2)()
            hi()
            hi()
            root_table()
            square_o(3)()
            root(3)
            for c in range(4):
                act.wait_ge(S("x_mix"), c + 1)
                square(4, c, X, O32)
            root(4)
            for c in range(4):
                norm_hi(3, c, O32, 48)

            def up(begin, n, prev):
                for u in range(begin, 4):
                    hi()
                if prev:
                    act.wait_ge(S("w_used"), pl.v + pl.ov - 4)
                    act.wait_ge(S("f2_act"), 2 * n)
                    act.activation(yH[:], tiles(act32), ACT.Copy).then_inc(S("f2_hi"), 1)
                for _ in range(8):
                    hi()
                act.wait_ge(S("w_used"), pl.v + pl.ov - 4)
                act.activation(gtmp, acc[:, pl.g % 2], ACT.Relu).then_inc(S("f2_relu"), 1)
                for _ in range(4):
                    hi()
                pl.g += 2

            def second(n, downs):
                if downs:
                    for _ in range(4):
                        hi()
                act.wait_ge(S("w_used"), pl.v + pl.ov - (4 if downs else 0))
                act.wait_ge(S("f2_act"), 2 * n + 1)
                act.activation(gtmp, acc[:, (pl.g + 1) % 2], ACT.Relu).then_inc(S("f2_relu"), 1)
                if downs:
                    for _ in range(12):
                        hi()
                    pl.g += 4

            up(4, 0, False)
            second(0, False)
            pl.phase("ffn2")
            up(0, 1, True)
            second(1, True)
            with act.Fori(0, 3) as i:
                pl.enter(i, 72, 64, 12, 1)
                for r in (2, 3):
                    pl.phase("ffn2")
                    up(0, i * 2 + r, True)
                    second(i * 2 + r, True)
            pl.leave(3, 72, 64, 12, 1)
            for _ in range(4):
                hi()
            act.wait_ge(S("f2_act"), 16)
            act.activation(hH[:, 0:8], tiles(act32), ACT.Copy).then_inc(S("f2_hi"), 1)
            for c, ahead in enumerate((10, 2, 0, 0)):
                for _ in range(ahead):
                    hi()
                if c == 3:
                    root_table()
                act.wait_ge(S("f2_sum"), 28 + c + 1)
                square(5, c, O32, tiles(blk(4, 2)))
            root(5)

        @block.tensor
        def _(pe):
            pl = Place()

            transposed = [0]

            def mm(o, l, r, start, stop):
                return pe.matmul(o, l, r, start=start, stop=stop, skip_group_check=True)

            def group(units, xh, xl, free, mode="A", k0=0, ready=None, hooks={}):
                for name, value in free:
                    pe.wait_ge(S(name), value)
                a = acc[:, pl.g % 2]
                for u in range(units):
                    if ready:
                        ready(u)
                    pe.wait_ge(S("unit_done"), pl.u + pl.ou + 1)
                    for k in range(KU):
                        kt = k0 + u * KU + k
                        first, last = u == 0 and k == 0, u == units - 1 and k == KU - 1
                        wh = whi[:, pl.v % NSPLIT, k * GCOL:(k + 1) * GCOL]
                        wl = wlo[:, pl.v % NSPLIT, k * GCOL:(k + 1) * GCOL]
                        for m in range({"A": GT, "AB": 2, "B": 0}[mode]):
                            o, c = a[:, m * T:(m + 1) * T], slice(m * P, (m + 1) * P)
                            mm(o, wh[:, c], xh[:, kt], first and m % 2 == 0, False)
                            mm(o, wh[:, c], xl[:, kt], False, False)
                            ins = mm(o, wl[:, c], xh[:, kt], False, last)
                        for t in range({"A": 0, "AB": TT, "B": TT}[mode]):
                            n = T if mode == "AB" else GCOL
                            at = GCOL + t * n if mode == "AB" else t * n
                            o, c, tk = a[:, at:at + n], slice(GCOL - n, GCOL), slice(t * P, (t + 1) * P)
                            mm(o, xh[:, kt, tk], wh[:, c], first and (mode == "B" or t == 0), False)
                            mm(o, xl[:, kt, tk], wh[:, c], False, False)
                            ins = mm(o, xh[:, kt, tk], wl[:, c], False, last)
                    ins.then_inc(S("w_used"), 1)
                    pl.u += 1
                    pl.v += 1
                    if pl.follows() and pl.past():
                        ada_sum()
                    if u in hooks:
                        hooks[u]()
                pl.g += 1

            def ada_sum():
                pe.wait_ge(S("unit_done"), pl.u + pl.ou)
                a = pl.a - 1
                if transposed[0] and not pl.looping:
                    pe.wait_ge(S("att_pt"), transposed[0])
                if a in (15, 20) and not pl.looping:
                    pe.wait_ge(S("mod_in"), 2 if a == 15 else 3)
                for m in range(GT):
                    o = modP[:, ds((a + pl.oa) * GT + m, 1)] if pl.looping else modP[:, a * GT + m:a * GT + m + 1]
                    for e in range(2):
                        ins = mm(o, adaacc[:, e, m * P:(m + 1) * P], one, e == 0, e == 1)
                ins.then_inc(S("ada_sum"), 1)

            def h_ready(index):
                def run(u):
                    if u % 2 == 0:
                        pe.wait_ge(S("h_lo"), 4 * index + u // 2 + 1)
                return run

            def norm_sum(k, c, sq, halved=True):
                q = sq[:, 4 * c:4 * c + 4]
                if halved:
                    pe.wait_ge(S("nm_half"), 4 * (k - 1) + c + 1 - (4 if k == 5 else 0))
                else:
                    pe.wait_ge(S("nm_sq"), 4 * k + c + 1)
                n = 2 if halved else 4
                for j in range(n):
                    ins = mm(W[:, 3, 0:T], C("mean"), q[:, j], c == 0 and j == 0, c == 3 and j == n - 1)
                if c == 3:
                    ins.then_inc(S("nm_sum"), 1)

            def level(l):
                def run():
                    if l == 0:
                        pe.wait_ge(S("f_in"), 2)
                        pe.wait_ge(S("q_in"), 2)
                        pe.wait_ge(S("mod_in"), 1)
                    else:
                        pe.wait_ge(S("c_done"), l)
                        pe.wait_ge(S("st_in"), l)
                    a, b = (ka, qa) if l == 0 else (Cb, Cb)
                    if l < 8:
                        for j in range(2 * H):
                            c = slice(j * P, (j + 1) * P)
                            ins = mm(Wf[:, c], a[:, c], b[:, c], True, True)
                    else:
                        for h in range(H):
                            ins = mm(Wf[:, h * P:(h + 1) * P], Cb[:, h * T:h * T + P], Cb[:, h * T + P:(h + 1) * T],
                                     True, True)
                    ins.then_inc(S("lvl"), 1)
                return run

            def hgrn_out():
                pe.wait_ge(S("off_in"), 1)
                pe.wait_ge(S("i_in"), 2)
                for h in range(H):
                    c = slice(h * P, (h + 1) * P)
                    mm(Wf[:, h * T:h * T + P], iav[:, 0, c], ST[:, h * T:h * T + P], True, True)
                    o = Wf[:, h * T + P:(h + 1) * T]
                    mm(o, iav[:, 0, c], off[:, c], True, False)
                    ins = mm(o, iav[:, 1, c], ST[:, h * T + P:(h + 1) * T], False, True)
                ins.then_inc(S("o_mm"), 1)

            def head_sum(k):
                def run():
                    pe.wait_ge(S("hn_sq"), k + 1)
                    if k:
                        pe.wait_ge(S("hn_done"), k)
                    for j in range(2 * H):
                        ins = mm(W[:, 3, j:j + 1], Cb[:, j * P:(j + 1) * P], C("head_mean", 1), True, True)
                    ins.then_inc(S("hn_sum"), 1)
                return run

            def head_spread(k):
                def run():
                    pe.wait_ge(S("hn_rec"), k + 1)
                    for j in range(2 * H):
                        ins = mm(Wf[:, j * P:(j + 1) * P], rr[:, 1, j:j + 1].to_broadcast([P, P]), ident, True, True)
                    ins.then_inc(S("hn_bc"), 1)
                return run

            def att(n, n0, n1):
                if n0 <= n - 3 < n1:
                    m = n - 3
                    kind, q, k, vs, y, head, fst, lst, gt = jobs[m]
                    pe.wait_ge(S("att_pt"), m + 1)
                    if m < N_B:
                        pe.wait_ge(S("vb_in"), 2)
                    elif m < N_N:
                        pe.wait_ge(S("kv_in"), 3)
                    else:
                        pe.wait_ge(S("vm_in"), 2)
                    if fst and head >= 2:
                        pe.wait_ge(S("att_y"), head - 1)
                    pt = pt2[:, m % 2]
                    o = W[:, 3, (head % 2) * T:(head % 2 + 1) * T]
                    ins = mm(o, vs[0], pt[:, 0:T], fst, False)
                    if len(vs) > 1:
                        ins = mm(o[:, P:T], vs[1], pt[:, T:3 * P], False, lst)
                    ins.then_inc(S("att_pv"), 1)
                if n0 <= n - 2 < n1:
                    m = n - 2
                    pe.wait_ge(S("att_p"), m + 1)
                    if m == N_B:
                        pe.wait_ge(S("gates_in"), 1)
                    elif m:
                        pe.wait_ge(S("att_pt"), m)
                    for j in range(parts(jobs[m][0])[1][1] // P):
                        ins = pe.transpose(W[:, 2, j * P:(j + 1) * P], sb3[:, m % 3, j * P:(j + 1) * P], ident)
                    transposed[0] = m + 1
                    ins.then_inc(S("att_t"), 1)
                if n0 <= n < n1:
                    kind, q, k = jobs[n][:3]
                    if n == 0:
                        pe.wait_ge(S("hn_done"), 3)
                        pe.wait_ge(S("hk_in"), 16)
                    elif n >= N_N:
                        pe.wait_ge(S("roped"), 15)
                    elif kind == "cmp":
                        pe.wait_ge(S("kvc_in"), 1)
                    elif n >= N_B:
                        pe.wait_ge(S("roped"), 6 if n == N_B else 7)
                        pe.wait_ge(S("kvc_in"), 1)
                    if n >= 2:
                        pe.wait_ge(S("att_max"), n - 1)
                    s = W[:, n % 2]
                    for t, (a, b) in enumerate(parts(kind)):
                        w = b - a
                        if kind == "bias":
                            hk = HK[:, jobs[n][5] * T + (P if t == 0 else 0):][:, 0:w]
                            mm(s[:, a:b], flip, hk, True, False)
                        ins = mm(s[:, a:b], q[:, t * P:(t + 1) * P], k[:, 0:w], kind != "bias", True)
                    ins.then_inc(S("att_s"), 1)

            def slot(n, n0, n1):
                return lambda: att(n, n0, n1)

            def also(*fs):
                return lambda: [f() for f in fs]

            pe.wait_ge(S("tables_in"), 32)
            pe.wait_ge(S("nm_first"), 1)
            mm(W[:, 3, 0:T], C("mean"), sq0[:, 0], True, True).then_inc(S("nm_sum"), 1)
            group(8, hH, hL, (), ready=h_ready(0))
            group(8, hH, hL, ())
            pl.phase("q_i")
            group(8, hH, hL, (("sig_f", 1),))
            group(8, hH, hL, (("sig_f", 2),))
            group(8, hH, hL, (("q_in", 1),), "B")
            group(8, hH, hL, (("q_in", 2),), "B")
            group(8, hH, hL, (("i_in", 1),), hooks={6: level(0)})
            group(8, hH, hL, (("i_in", 2),), hooks={6: level(1)})
            group(8, hH, hL, (("g_in", 1),), hooks={6: level(2)})
            group(8, hH, hL, (("g_in", 2),), hooks={6: level(3)})
            group(8, hH, hL, (("qk_in", 1),), hooks={6: level(4)})
            group(8, hH, hL, (("qk_in", 2),), hooks={6: level(5)})
            group(8, hH, hL, (("qk_in", 3),), "B", hooks={6: level(6)})
            group(8, hH, hL, (("qk_in", 4),), "B", hooks={6: level(7)})
            group(8, hH, hL, (("vb_in", 1),), hooks={6: level(8)})
            group(8, hH, hL, (("vb_in", 2),), hooks={1: hgrn_out, 4: head_sum(0), 7: head_spread(0)})
            group(8, hH, hL, (("gate_in", 1),), hooks={1: head_sum(1), 4: head_spread(1), 6: head_sum(2)})
            group(8, hH, hL, (("gate_in", 2),), hooks={1: head_spread(2), 7: slot(0, 0, N_B)})

            def y_ready(index):
                def run(u):
                    if u == 0:
                        pe.wait_ge(S("y_lo"), index)
                return run
            for i in range(4):
                group(4, yH, yL, (("gate_in", 3 + i) if i < 2 else ("pa_in", i - 1),), ready=y_ready(1),
                      hooks={3: slot(i + 1, 0, N_B)})
            for i in range(4):
                group(8, hH, hL, (("pa_in", 3 + i) if i < 2 else ("gate_in", 5 + i - 2),),
                      hooks={3: slot(5 + 2 * i, 0, N_B), 7: slot(6 + 2 * i, 0, N_B)})
            for i in range(4):
                group(4, yH, yL, (("gate_in", 7 + i) if i < 2 else ("pb_in", i - 1),), ready=y_ready(2))

            def merged_ready(u):
                if u % 2 == 0:
                    pe.wait_ge(S("m_lo"), u // 2 + 1)
            pl.phase("out")
            for i in range(4):
                hooks = {6: lambda: norm_sum(1, i - 1, tiles(M))} if i else {}
                group(8, hH, hL, (("pb_in", 3 + i) if i < 2 else ("x1", i - 1),), ready=merged_ready, hooks=hooks)

            norm_sum(1, 3, tiles(M))

            def ffn1(n, free, down):
                pl.phase("ffn1" if down else "ffn1_first")
                group(8, hH, hL, free[0:1], ready=None if down else h_ready(1))
                group(8, hH, hL, free[1:2])
                if down:
                    down1(n, (("ff_g", n + 1), ("ff_act", n + 1)))

            def down1(n, free, last=False):
                pe.wait_ge(S("ff_lo"), n)
                for g in range(4):
                    if last and g == 3:
                        norm_sum(2, 0, O32)
                    group(2, yH, yL, k0=GT if last else 0, free=free[g:g + 1] if g < 2 else (("ff_sum", (n - 1) * 4 + g - 1),))

            ffn1(0, (("x1", 3), ("x1", 4)), False)
            ffn1(1, (("ff_g", 1), ("ff_act", 1)), True)
            with pe.Fori(0, 9) as i:
                pl.enter(i, 32, 24, 6, 1)
                ffn1(i + 2, (("ff_sum", i * 4 + 3), ("ff_sum", i * 4 + 4)), True)
            pl.leave(9, 32, 24, 6, 1)
            down1(11, (("ff_sum", 39), ("ff_sum", 40)), last=True)

            for c in range(1, 4):
                norm_sum(2, c, O32)

            def rotate(n, g, c0):
                def run():
                    pe.wait_ge(S("rope_raw"), n + 1)
                    mm(acc[:, g % 2, c0:c0 + GCOL], swap, rope, True, True).then_inc(S("rope_swap"), 1)
                return run
            gg = PHASES["cmp_kv"][1]
            group(8, hH, hL, (("ff_sum", 43),), ready=h_ready(2))
            pl.phase("qn")
            group(8, hH, hL, (("ff_sum", 44),), hooks={2: rotate(0, gg, 0)})
            group(8, hH, hL, (("roped", 1), ("kv_in", 1)), hooks={2: rotate(1, gg + 1, 0), 5: rotate(2, gg + 1, GCOL)})

            def cmp_unit(kind, u):
                def run():
                    if u == 0:
                        pe.wait_ge(S("cx_lo"), kind + 1)
                    pe.wait_ge(S("unit_done"), pl.u + 1)
                    for k in range(8):
                        c, x = slice(k * P, (k + 1) * P), cxp[kind][:, u * 8 + k]
                        wh, wl = whi[:, pl.v % NSPLIT, c], wlo[:, pl.v % NSPLIT, c]
                        mm(hidP[:, kind, 0:60], wh, x.rearrange("p e c -> p (e c)"), u == 0 and k == 0, False)
                        ins = mm(hidP[:, kind, 0:30], wl, x[:, 0], False, u == 3 and k == 7)
                    ins.then_inc(S("w_used"), 1)
                    pl.u += 1
                    pl.v += 1
                return run

            def gates_mm():
                pe.wait_ge(S("wg_lo"), 1)
                pe.wait_ge(S("mod_in"), 2)
                for k in range(KT):
                    o = W[0:N_GATE, 2, 0:T]
                    mm(o, wgh[:, k], hH[:, k], k == 0, False)
                    mm(o, wgh[:, k], hL[:, k], False, False)
                    ins = mm(o, wgl[:, k], hH[:, k], False, k == KT - 1)
                ins.then_inc(S("gates_mm"), 1)

            def gates_turn():
                pe.wait_ge(S("gates_sig"), 1)
                for t in range(TT):
                    ins = pe.transpose(W[:, 2, t * N_GATE:(t + 1) * N_GATE], gateT[:, t * P:(t + 1) * P],
                                       ident[0:N_GATE, 0:N_GATE])
                ins.then_inc(S("gates_turn"), 1)

            def compressed():
                pe.wait_ge(S("hid_in"), 1)
                mm(W[:, 0, 0:T], w2[:, 0], hid[:, 0].rearrange("p g c -> p (g c)"), True, True)
                for g in range(2):
                    ins = mm(W[:, 0, T + g * P:T + (g + 1) * P], hid[:, 1, g], w2[:, 1], True, True)
                ins.then_inc(S("cmp_kv"), 1)
            also_sel = {0: gates_mm, 1: rotate(3, gg + 2, 0), 4: rotate(4, gg + 2, GCOL), 5: gates_turn}
            hooks = {u: also(cmp_unit(u // 4, u % 4), also_sel.get(u, lambda: None)) for u in range(8)}
            group(8, hH, hL, (("roped", 3),), "AB", hooks=hooks)
            group(8, hH, hL, (("roped", 5),), "AB", hooks={2: rotate(5, gg + 3, 0), 5: compressed})
            pl.phase("moba")
            n = N_B
            frees = ((("roped", 6), ("kv_in", 2)), (("roped", 7), ("kv_in", 3)), (("roped", 9),), (("roped", 11),),
                     (("roped", 13),), (("roped", 15),))
            for j in range(6):
                hooks = {}
                for u in ((0, 3, 4, 6) if j == 0 else (0, 2, 4, 6)):
                    hooks[u] = slot(n, N_B, N_N)
                    n += 1
                if j == 5:
                    for u in (5, 6, 7):
                        hooks[u] = slot(n - 1, N_B, N_N)
                        n += 1
                    n -= 1
                    hooks[7] = also(hooks[7], slot(n, N_B, N_N))
                if j == 0:
                    hooks[2] = rotate(6, gg + 4, 0)
                elif j <= 4:
                    r = 7 + 2 * (j - 1)
                    first = rotate(r, gg + 4 + j, 0)
                    hooks[2] = also(first, hooks[2])
                    hooks[5] = rotate(r + 1, gg + 4 + j, GCOL)
                group(8, hH, hL, frees[j], "B" if j >= 4 else "A", hooks=hooks)
            assert n == N_N + 2
            n = N_N
            frees = (("vm_in", 1), ("vm_in", 2), ("wo_in", 1), ("wo_in", 2))
            for i, at in enumerate(((2, 3), (0, 2, 3), (0, 2, 3), (0, 2, 3))):
                hooks = {}
                for u in at:
                    hooks[u] = slot(n, N_N, N_M)
                    n += 1
                group(4, yH, yL, frees[i:i + 1], ready=y_ready(3), hooks=hooks)
            assert n == N_M + 3
            frees = (("wo_in", 3), ("wo_in", 4), ("o_sum", 1), ("o_sum", 2))

            pl.phase("wo")

            def om_ready(u):
                if u == 0:
                    pe.wait_ge(S("om_lo"), 1)
            for i in range(4):
                hooks = {1: lambda: norm_sum(3, i - 2, tiles(blk(4, 2)))} if i >= 2 else {}
                group(4, hH, hL, frees[i:i + 1], ready=om_ready, hooks=hooks)
            for c in (2, 3):
                norm_sum(3, c, tiles(blk(4, 2)))
            for c in range(4):
                norm_sum(4, c, O32, halved=False)

            def down2(n, free, last=False):
                pe.wait_ge(S("f2_lo"), n)
                for g in range(4):
                    hooks = {c + 1: lambda c=c: norm_sum(5, c, tiles(blk(4, 2))) for c in range(2)} if last and g == 3 \
                        else {}
                    group(4, hH if last else yH, hL if last else yL, free[g:g + 1] if g < 2 else (("f2_sum", (n - 1) * 4 + g - 1),), hooks=hooks)

            def ffn2(n, free, down):
                pl.phase("ffn2" if down else "ffn2_first")
                group(8, hH, hL, free[0:1], ready=None if down else h_ready(3))
                group(8, hH, hL, free[1:2])
                if down:
                    down2(n, (("f2_relu", 2 * n + 1), ("f2_relu", 2 * n + 2)))

            ffn2(0, (("o_sum", 3), ("o_sum", 4)), False)
            ffn2(1, (("f2_relu", 1), ("f2_relu", 2)), True)
            with pe.Fori(0, 3) as i:
                pl.enter(i, 72, 64, 12, 1)
                for r in range(2):
                    ffn2(i * 2 + (r + 2), (("f2_sum", i * 8 + (4 * r + 3)), ("f2_sum", i * 8 + (4 * r + 4))), True)
            pl.leave(3, 72, 64, 12, 1)
            down2(8, (("f2_sum", 27), ("f2_sum", 28)), last=True)
            for c in (2, 3):
                norm_sum(5, c, tiles(blk(4, 2)))

        @block.vector
        def _(dve):
            pl = Place()
            steps, mods, ada_last = [0], [0], [0]

            def then(ins):
                steps[0] += 1
                ins.then_inc(S("dve_step"), 1)
                dve.wait_ge(S("dve_step"), steps[0])

            def lo(n=1):
                for _ in range(n):
                    s, v = pl.u % NRAW, pl.v % NSPLIT
                    dve.wait_ge(S("w_hi"), pl.v + pl.ov + 1)
                    dve.tensor_tensor(wlo[:, v], raw[:, s], whi[:, v].bitcast(F32), ALU.subtract)\
                       .then_inc(S("unit_done"), 1)
                    pl.u += 1
                    pl.v += 1
                    if pl.follows():
                        ada_unit()

            def ada_unit():
                s = pl.u % NRAW
                dve.wait_ge(landed[s], 16 * (pl.u // NRAW + 1) + pl.ou * (16 // NRAW))
                for e in range(2):
                    w, c, o = raw[:, s, e * GCOL:(e + 1) * GCOL], cs[:, 2 * pl.j + e:2 * pl.j + e + 1], adaacc[:, e]
                    if pl.j == 0:
                        if e == 0 and pl.a:
                            dve.wait_ge(S("ada_sum"), pl.a + pl.oa)
                        ins = dve.tensor_scalar(o, w, c, None, ALU.mult)
                    else:
                        if e == 0:
                            dve.wait_ge(S("ada_even"), pl.a * 8 + pl.j + pl.oa * 8)
                        else:
                            dve.wait_ge(S("unit_done"), ada_last[0] + pl.ou)
                        ins = dve.scalar_tensor_tensor(out=o, in0=w, scalar=c, in1=o, op0=ALU.mult, op1=ALU.add)
                    ins.then_inc(S("unit_done") if e else S("ada_even"), 1)
                ada_last[0] = pl.u + 1
                pl.past()

            def modulation(n, c0, c1):
                dve.wait_ge(S("ada_sum"), n)
                dve.tensor_tensor(mod[:, c0:c1], modP[:, c0:c1], V("b_ada", c1 - c0, c0), ALU.add)\
                   .then_inc(S("mod_in"), 1)
                mods[0] += 1
                dve.wait_ge(S("mod_in"), mods[0])

            def scaled(a, gain, scale, add):
                return dve.scalar_tensor_tensor(out=modA[:, a], in0=mod[:, scale:scale + 16], scalar=add,
                                                in1=V(gain, 16), op0=ALU.add, op1=ALU.mult)

            def group(units=8, hooks={}, begin=0):
                for u in range(begin, units):
                    lo()
                    if u in hooks:
                        hooks[u]()
                pl.g += 1

            def halve(k, c, sq):
                dve.wait_ge(S("nm_sq"), 4 * k + c + 1)
                a, b = sq[:, 4 * c:4 * c + 2], sq[:, 4 * c + 2:4 * c + 4]
                dve.tensor_tensor(a, a, b, ALU.add).then_inc(S("nm_half"), 1)

            def norm_rstd(k):
                dve.wait_ge(S("nm_root"), k + 1)
                then(dve.reciprocal(rstd[:], rstd[:]))

            def h_low(index, h32, c, shift=None):
                dve.wait_ge(S("h_hi"), 4 * index + c + 1)
                if shift is None:
                    q = slice(4 * c, 4 * c + 4)
                    ins = dve.tensor_tensor(hL[:, q], h32[:, q], hH[:, q].bitcast(F32), ALU.subtract)
                else:
                    for j in range(4 * c, 4 * c + 4):
                        ins = dve.scalar_tensor_tensor(out=hL[:, j], in0=h32[:, j], scalar=mod[:, shift + j:shift + j + 1],
                                                       in1=hH[:, j].bitcast(F32), op0=ALU.add, op1=ALU.subtract)
                ins.then_inc(S("h_lo"), 1)

            def norm_h(index, x, h32, gain, shift=None, between=None):
                for c in range(4):
                    for j in range(4 * c, 4 * c + 4):
                        ins = dve.scalar_tensor_tensor(out=h32[:, j], in0=x[:, j], scalar=gain[:, j:j + 1], in1=rstd[:],
                                                       op0=ALU.mult, op1=ALU.mult)
                    ins.then_inc(S("h_ready"), 1)
                    if c:
                        h_low(index, h32, c - 1, shift)
                        if between:
                            between()
                h_low(index, h32, 3, shift)
                if between:
                    between()

            def edges():
                dve.wait_ge(S("ext_in"), 16)
                dve.tensor_copy(ext[:, 0:P], ext[:, P:P + 1].to_broadcast([H, P])).then_inc(S("ext_full"), 1)
                e = P + N_REL
                dve.tensor_copy(ext[:, e:EXT], ext[:, e - 1:e].to_broadcast([H, EXT - e])).then_inc(S("ext_full"), 1)

            for c in range(4):
                dve.wait_ge(S("nm_sq"), c + 1)
                then(dve.tensor_tensor(sq0[:, 4 * c:4 * c + 2], sq0[:, 4 * c:4 * c + 2], sq0[:, 4 * c + 2:4 * c + 4],
                                       ALU.add))
                if c:
                    then(dve.tensor_tensor(sq0[:, 0:2], sq0[:, 0:2], sq0[:, 4 * c:4 * c + 2], ALU.add))
            dve.tensor_tensor(sq0[:, 0], sq0[:, 0], sq0[:, 1], ALU.add).then_inc(S("nm_first"), 1)
            dve.wait_ge(S("tables_in"), 32)
            norm_rstd(0)
            norm_h(0, x0, sq0, V("norm_mix", KT), between=lo)
            l0, l1 = V("lb", H), V("lb", H, H)
            then(dve.tensor_tensor(lb[:, 2], l0, l1, ALU.max))
            dve.tensor_tensor(lb[:, 0], l0, lb[:, 2], ALU.subtract)
            dve.tensor_tensor(lb[:, 1], l1, lb[:, 2], ALU.subtract).then_inc(S("lb_step"), 1)

            def bounds():
                then(dve.tensor_scalar(q_scale[:], V("q_gain"), SCALE, None, ALU.mult))
                dve.wait_ge(S("lb_exp"), 1)
                then(dve.tensor_tensor(lb[:, 2], lb[:, 0], lb[:, 1], ALU.add))
                then(dve.reciprocal(lb[:, 3], lb[:, 2]))
                then(dve.tensor_tensor(lb[:, 4], lb[:, 0], lb[:, 3], ALU.mult))
                then(dve.tensor_scalar(lb[:, 5], lb[:, 4], -1.0, 1.0, ALU.mult, ALU.add))
                dve.wait_ge(S("c_sig"), 1)
                then(dve.tensor_tensor(cs[:], cs[:], V("c", 16), ALU.mult))

            def masks():
                dve.wait_ge(S("mask_in"), 16)
                then(dve.tensor_copy(lmask[:], lmaskf))

            def half(b, i):
                return b[:, i * 1024:(i + 1) * 1024]

            def forget(i):
                def run():
                    dve.wait_ge(S("sig_f"), i + 1)
                    for h in range(4 * i, 4 * i + 4):
                        c = slice(h * T, (h + 1) * T)
                        ins = dve.tensor_scalar(Cb[:, c], ka[:, c], lb[:, 5, h:h + 1], lb[:, 4, h:h + 1],
                                                ALU.mult, ALU.add)
                    then(ins)
                    dve.tensor_scalar(half(ka, i), half(Cb, i), -1.0, 1.0, ALU.mult, ALU.add)
                    dve.tensor_scalar(half(Cb, i), half(Cb, i), 2.0 ** -63, None, ALU.max).then_inc(S("f_in"), 1)
                return run

            def silu_q(i):
                def run():
                    dve.wait_ge(S("sig_q"), i + 1)
                    dve.tensor_tensor(half(qa, i), half(qa, i), acc[:, (2 + i) % 2], ALU.mult).then_inc(S("q_in"), 1)
                return run

            def silu_g(i):
                def run():
                    dve.wait_ge(S("sig_g"), i + 1)
                    for h in range(4):
                        c = slice((4 * i + h) * T, (4 * i + h + 1) * T)
                        ins = dve.scalar_tensor_tensor(out=ga[:, c], in0=ga[:, c], scalar=V("out_gain", 1, 4 * i + h),
                                                       in1=acc[:, (6 + i) % 2, h * T:(h + 1) * T],
                                                       op0=ALU.mult, op1=ALU.mult)
                    ins.then_inc(S("g_in"), 1)
                return run

            def scan():
                dve.wait_ge(S("ln_f"), 1)
                for j in range(2 * H):
                    c = slice(j * P, (j + 1) * P)
                    ins = dve.tensor_tensor_scan(bc[:, c], ones, Cb[:, c], 0.0, ALU.mult, ALU.add)
                then(ins)

            def take(l):
                dve.wait_ge(S("lvl"), l + 1)
                if l == 0:
                    dve.wait_ge(S("st_zero"), 1)
                mask = lmask[:, l * P:(l + 1) * P].unsqueeze(1).to_broadcast([P, 2 * H, P])
                dve.copy_predicated(ST.rearrange("p (j t) -> p j t", t=P), mask, Wf.rearrange("p (j t) -> p j t", t=P))\
                   .then_inc(S("st_in"), 1)

            def diff(l):
                if l < 8:
                    b = 1 << (l - 1)
                    v = bc.rearrange("p (n b) -> p n b", b=2 * b)
                    dve.tensor_tensor(Cb.rearrange("p (n b) -> p n b", b=2 * b), v,
                                      v[:, :, b - 1:b].to_broadcast([P, BLK // (2 * b), 2 * b]), ALU.subtract)\
                       .then_inc(S("c_diff"), 1)
                else:
                    v = bc.rearrange("p (h t s) -> p h t s", h=H, t=TT)[:, :, 0]
                    dve.tensor_tensor(Cb.rearrange("p (h t s) -> p h t s", h=H, t=TT)[:, :, 0], v,
                                      v[:, :, P - 1:P].to_broadcast([P, H, P]), ALU.subtract).then_inc(S("c_diff"), 1)

            def prepare(l):
                def run():
                    take(l - 1)
                    diff(l)
                return run

            def decayed(l):
                def run():
                    dve.wait_ge(S("c_exp"), l)
                    b = 1 << (l - 1) if l < 8 else P
                    v, kv, qv = (x.rearrange("p (n h b) -> p n h b", h=2, b=b) for x in (Cb, ka, qa))
                    dve.tensor_tensor(v[:, :, 0], v[:, :, 0], kv[:, :, 0], ALU.mult)
                    dve.tensor_tensor(v[:, :, 1], v[:, :, 1], qv[:, :, 1], ALU.mult).then_inc(S("c_done"), 1)
                return run

            group(begin=4, hooks={6: bounds})
            group(hooks={1: edges, 2: masks, 5: forget(0)})
            pl.phase("q_i")
            group(hooks={5: forget(1)})
            group(hooks={5: silu_q(0)})
            group(hooks={5: silu_q(1)})
            group(hooks={3: scan})
            group(hooks={3: lambda: modulation(2, 0, 8)})
            group(hooks={4: silu_g(0), 5: prepare(1), 7: decayed(1)})
            group(hooks={4: silu_g(1), 5: prepare(2), 7: decayed(2)})
            for l in range(3, 9):
                group(hooks={5: prepare(l), 7: decayed(l)})

            def head_rec(k):
                def run():
                    dve.wait_ge(S("hn_root"), k + 1)
                    dve.reciprocal(rr[:, 1], rr[:, 0]).then_inc(S("hn_rec"), 1)
                return run

            def head_apply(k):
                def run():
                    if k == 0:
                        dve.wait_ge(S("o_in"), 1)
                        dve.wait_ge(S("hn_sq"), 1)
                        then(dve.tensor_tensor(ob, ob, ga, ALU.mult))
                        dve.wait_ge(S("hn_bc"), 1)
                        dve.tensor_tensor(ob, ob, Wf, ALU.mult).then_inc(S("hn_done"), 1)
                    else:
                        x, g = ((qb, q_scale[:]), (kb, V("k_gain")))[k - 1]
                        dve.wait_ge(S("hn_bc"), k + 1)
                        dve.scalar_tensor_tensor(out=x, in0=x, scalar=g, in1=Wf, op0=ALU.mult, op1=ALU.mult)\
                           .then_inc(S("hn_done"), 1)
                return run

            def y_low(n, src):
                dve.wait_ge(S("y_hi"), n)
                dve.tensor_tensor(yL[:], tiles(src), yH[:].bitcast(F32), ALU.subtract).then_inc(S("y_lo"), 1)

            def also(*fs):
                return lambda: [f() for f in fs]

            group()
            group(hooks={0: head_rec(0), 3: head_apply(0), 5: also(lambda: y_low(1, ob), head_rec(1))})
            group(hooks={0: head_apply(1), 2: head_rec(2), 5: head_apply(2)})

            def att(n, n0, n1):
                if n0 <= n - 1 < n1:
                    m = n - 1
                    kind, gt = jobs[m][0], jobs[m][8]
                    r = m % 3
                    dve.wait_ge(S("att_exp"), m + 1)
                    then(dve.tensor_scalar(stat[:, 3, r], stat[:, 2, r], TINY, None, ALU.max))
                    then(dve.reciprocal(stat[:, 3, r], stat[:, 3, r]))
                    if m == N_B:
                        dve.wait_ge(S("gates_in"), 1)
                    for t, (a, b) in enumerate(parts(kind)):
                        p, s = sb3[:, r, a:b], stat[:, 3, r, t:t + 1]
                        if gt:
                            ins = dve.tensor_scalar(p, p, s, gt[t], ALU.mult, ALU.mult)
                        else:
                            ins = dve.tensor_scalar(p, p, s, None, ALU.mult)
                    ins.then_inc(S("att_p"), 1)
                if n0 <= n < n1:
                    kind, r = jobs[n][0], n % 3
                    dve.wait_ge(S("att_s"), n + 1)
                    if n >= 3:
                        dve.wait_ge(S("att_t"), n - 2)
                    for t, (a, b) in enumerate(parts(kind)):
                        ins = dve.tensor_tensor_reduce(sb3[:, r, a:b], W[:, n % 2, a:b], mask_of(kind, t), 1.0,
                                                       MAX_FLOOR, ALU.add, ALU.max, stat[:, 0, r, t:t + 1])
                    ins.then_inc(S("att_max"), 1)
                    dve.wait_ge(S("att_max"), n + 1)
                    dve.tensor_scalar(stat[:, 1, r], stat[:, 0, r], -1.0 if kind == "bias" else -SCALE, None, ALU.mult)\
                       .then_inc(S("att_neg"), 1)

            def slot(n, n0, n1):
                return lambda: att(n, n0, n1)

            def by_gate_a(i):
                def run():
                    m = half(M, i)
                    dve.wait_ge(S("gate_in"), i + 1)
                    dve.wait_ge(S("w_used"), PHASES["proj_a"][0] + 4 * (i + 1))
                    dve.tensor_tensor(m, m, acc[:, (PHASES["proj_a"][1] + i) % 2], ALU.mult).then_inc(S("pa_in"), 1)
                return run

            def by_gate_b(i):
                def run():
                    g = half(sgb, i)
                    dve.wait_ge(S("gate_in"), i + 5)
                    dve.wait_ge(S("w_used"), PHASES["proj_b"][0] + 4 * (i + 1))
                    dve.tensor_tensor(g, g, acc[:, (PHASES["proj_b"][1] + i) % 2], ALU.mult).then_inc(S("pb_in"), 1)
                    dve.wait_ge(S("pb_in"), i + 1)
                    dve.wait_ge(S("pa_in"), i + 1)
                    dve.tensor_tensor(half(M, i), half(M, i), g, ALU.add).then_inc(S("merged"), 1)
                return run

            group(4, hooks={2: slot(0, 0, N_B)})
            for i in range(1, 4):
                group(4, hooks={2: slot(i, 0, N_B), 3: by_gate_a(i - 1)})
            for i in range(4):
                hooks = {2: slot(4 + 2 * i, 0, N_B), 6: slot(5 + 2 * i, 0, N_B)}
                if i == 0:
                    hooks[3] = by_gate_a(3)
                if i == 3:
                    hooks[7] = lambda: y_low(2, yb)
                group(hooks=hooks)

            def merged_low(c):
                q = slice(4 * c, 4 * c + 4)
                dve.wait_ge(S("m_hi"), c + 1)
                dve.tensor_tensor(hL[:, q], tiles(M)[:, q], hH[:, q].bitcast(F32), ALU.subtract).then_inc(S("m_lo"), 1)
            group(4)
            group(4, hooks={3: by_gate_b(0)})
            for i in range(2, 4):
                group(4, hooks={2: lambda: merged_low(i - 2), 3: by_gate_b(i - 1)})

            def add_x(i):
                def run():
                    if i == 0:
                        dve.wait_ge(S("x_again"), 16)
                    dve.wait_ge(S("w_used"), PHASES["out"][0] + 8 * (i + 1))
                    x = X[:, 4 * i:4 * i + 4]
                    dve.tensor_tensor(x, x, tiles(acc[:, (PHASES["out"][1] + i) % 2]), ALU.add).then_inc(S("x1"), 1)
                return run
            pl.phase("out")
            lo(3)
            merged_low(2)
            lo(1)
            by_gate_b(3)()
            merged_low(3)
            lo(4)
            pl.g += 1
            for i in range(1, 4):
                group(hooks={3: add_x(i - 1), 6: lambda: halve(1, i - 1, tiles(M))})
            pl.phase("ffn1_first")
            lo(4)
            add_x(3)()
            halve(1, 3, tiles(M))
            norm_rstd(1)
            norm_h(1, X, tiles(M), V("norm_ffn", KT))

            def product_low(n, q=slice(0, GT)):
                dve.wait_ge(S("ff_hi"), n)
                dve.tensor_tensor(yL[:, q], tiles(act32[:, 0:1024]), yH[:, q].bitcast(F32), ALU.subtract)\
                   .then_inc(S("ff_lo"), 1)

            def add_down(g, n, v):
                dve.wait_ge(S("w_used"), v)
                dve.wait_ge(S("ff_sum"), (n - 1) * 4 + g) if not isinstance(n, int) or (n - 1) * 4 + g > 0 else None
                x = X[:, 4 * g:4 * g + 4]
                dve.tensor_tensor(x, x, tiles(acc[:, (PHASES["ffn1"][1] + g) % 2]), ALU.add).then_inc(S("ff_sum"), 1)

            def ffn1(n, begin, before, down):
                here = lambda: pl.v + pl.ov
                if down:
                    pl.phase("ffn1")
                if before:
                    lo(2)
                    add_down(2, n - 1, here() - 4)
                    lo(2)
                    add_down(3, n - 1, here() - 4)
                    product_low(n)
                    lo(4)
                else:
                    if down:
                        lo(4)
                        product_low(n)
                        lo(4)
                    else:
                        lo(8 - begin)
                lo(4)
                dve.wait_ge(S("ff_sig"), n + 1)
                dve.tensor_tensor(gtmp, gtmp, acc[:, PHASES["ffn1"][1] % 2], ALU.mult).then_inc(S("ff_g"), 1)
                lo(4)
                if down:
                    lo(4)
                dve.wait_ge(S("w_used"), here() - (4 if down else 0))
                dve.wait_ge(S("ff_g"), n + 1)
                dve.tensor_tensor(act32[:, 0:1024], gtmp, acc[:, (PHASES["ffn1"][1] + 1) % 2], ALU.mult)\
                   .then_inc(S("ff_act"), 1)
                if down:
                    lo(2)
                    add_down(0, n, here() - 4)
                    lo(2)
                    add_down(1, n, here() - 4)

            ffn1(0, 4, False, False)
            ffn1(1, 0, False, True)
            with dve.Fori(0, 9) as i:
                pl.enter(i, 32, 24, 6, 1)
                ffn1(i + 2, 0, True, True)
            pl.leave(9, 32, 24, 6, 1)
            lo(2)
            add_down(2, 10, pl.v - 4)
            lo(2)
            product_low(11, slice(GT, 2 * GT))
            add_down(3, 10, pl.v - 4)
            lo(2)
            add_down(0, 11, pl.v - 4)
            lo(2)
            add_down(1, 11, pl.v - 4)
            modulation(15, 8, 60)
            scaled(0, "pre_mix", 16, 1.0)
            then(scaled(1, "post_mix", 32, 0.0))
            halve(2, 0, O32)
            lo(2)
            add_down(2, 11, pl.v - 4)
            halve(2, 1, O32)
            lo(2)
            add_down(3, 11, pl.v - 4)
            halve(2, 2, O32)
            halve(2, 3, O32)
            norm_rstd(2)
            norm_h(2, X, O32, modA[:, 0], 0)
            dve.wait_ge(S("wg_hi"), 1)
            dve.tensor_tensor(wgl[:], wg, wgh[:].bitcast(F32), ALU.subtract).then_inc(S("wg_lo"), 1)

            def rotated(n, g, c0, dst):
                def run():
                    tab = lambda name: C(name, T).unsqueeze(1).to_broadcast([P, 2, T])
                    r, d = tiles(rope), tiles(dst)
                    dve.wait_ge(S("rope_swap"), n + 1)
                    then(dve.tensor_tensor(d, r, tab("cos"), ALU.mult))
                    then(dve.tensor_tensor(r, tiles(acc[:, g % 2, c0:c0 + GCOL]), tab("sin"), ALU.mult))
                    dve.tensor_tensor(d, d, r, ALU.add).then_inc(S("roped"), 1)
                return run

            def blocks(kind):
                def run():
                    if kind == 0:
                        dve.wait_ge(S("roped"), 1)
                    else:
                        dve.wait_ge(S("kv_in"), 1)
                    base = arena[:, 0:1]
                    src = bass.AP(base.tensor, base.offset + kind * 2 * T,
                                  [list(base.ap[0]), [1, CMP_LEN], [T, 2], [CMP_STRIDE, N_CMP]])
                    pos = V("v_pos" if kind else "k_pos", CMP_LEN)
                    pos = bass.AP(pos.tensor, pos.offset, [list(pos.ap[0]), [1, CMP_LEN], [0, 2], [0, N_CMP]])
                    o = cx[:, kind * 1024:kind * 1024 + 960].rearrange("p (l g c) -> p l g c", g=2, c=N_CMP)
                    dve.tensor_tensor(o, src, pos, ALU.add).then_inc(S("cx"), 1)
                return run

            def blocks_low(kind):
                def run():
                    src = cx[:, kind * 1024:kind * 1024 + 960].rearrange("p (l c) -> p l c", c=30)
                    dve.wait_ge(S("cx_hi"), kind + 1)
                    dve.tensor_tensor(cxp[kind][:, :, 1], src, cxp[kind][:, :, 0].bitcast(F32), ALU.subtract)\
                       .then_inc(S("cx_lo"), 1)
                return run

            def hidden_sum():
                dve.wait_ge(S("w_used"), PHASES["selwin"][0] + 16)
                then(dve.tensor_copy(hsum, hidP[:, :, 30:60]))
                dve.tensor_tensor(hsum, hsum, hidP[:, :, 0:30], ALU.add).then_inc(S("hid_sum"), 1)

            def hidden():
                dve.wait_ge(S("hid_sig"), 1)
                dve.wait_ge(S("hid_zero"), 1)
                for k in range(2):
                    g = lambda x: x.rearrange("p (g c) -> p g c", g=2)
                    ins = dve.tensor_tensor(hid[:, k, :, 0:N_CMP], g(hsg[:, k]), g(hsum[:, k]), ALU.mult)
                ins.then_inc(S("hid_in"), 1)

            gg = PHASES["cmp_kv"][1]
            group(begin=4)
            pl.phase("qn")
            group(hooks={5: rotated(0, gg, 0, arena[:, 0:GCOL])})
            group(hooks={1: blocks(0), 2: blocks(1), 5: rotated(1, gg + 1, 0, qn[:, 0:GCOL]),
                         6: blocks_low(0), 7: blocks_low(1)})
            for u in range(8):
                lo(2)
                if u == 0:
                    rotated(2, gg + 1, GCOL, qn[:, GCOL:2 * GCOL])()
                if u == 3:
                    rotated(3, gg + 2, 0, qn[:, 2 * GCOL:3 * GCOL])()
                if u == 6:
                    rotated(4, gg + 2, GCOL, qn[:, 3 * GCOL:4 * GCOL])()
            pl.g += 1
            group(hooks={3: hidden_sum, 5: also(hidden, rotated(5, gg + 3, 0, arena[:, 1024:1536]))})
            pl.phase("moba")
            n = N_B
            dst = [qm[:, i * GCOL:(i + 1) * GCOL] for i in range(4)] + [km[:, i * GCOL:(i + 1) * GCOL] for i in range(4)]
            for j in range(6):
                hooks = {}
                for u in ((3, 6, 7) if j == 0 else (1, 3, 5, 7)):
                    hooks[u] = slot(n, N_B, N_N)
                    n += 1
                if j == 0:
                    hooks[4] = rotated(6, gg + 4, 0, arena[:, 1536:2048])
                else:
                    r = 7 + 2 * (j - 1)
                    if j <= 4:
                        hooks[5] = also(rotated(r, gg + 4 + j, 0, dst[r - 7]), hooks[5])
                    if j >= 2:
                        hooks[0] = rotated(r - 1, gg + 3 + j, GCOL, dst[r - 8])
                group(hooks=hooks)
            for u in range(4):
                lo(1)
                att(n + u, N_B, N_N)
            y_low(3, on)
            pl.g += 1
            n = N_N
            for i in range(1, 4):
                group(4, hooks={1: slot(n, N_N, N_M), 2: slot(n + 1, N_N, N_M), 3: slot(n + 2, N_N, N_M)})
                n += 3
            pl.phase("wo")
            lo(2)
            att(n, N_N, N_M)
            lo(2)
            att(n + 1, N_N, N_M)
            dve.wait_ge(S("om_hi"), 1)
            dve.tensor_tensor(hL[:, 0:8], tiles(om), hH[:, 0:8].bitcast(F32), ALU.subtract).then_inc(S("om_lo"), 1)
            pl.g += 1

            def wo_add(i):
                def run():
                    dve.wait_ge(S("wo_in"), i + 1)
                    dve.wait_ge(S("w_used"), PHASES["wo"][0] + 16 + 4 * (i + 1))
                    o = O32[:, 4 * i:4 * i + 4]
                    dve.tensor_tensor(o, o, tiles(acc[:, (PHASES["wo"][1] + i) % 2]), ALU.add).then_inc(S("o_sum"), 1)
                return run
            group(4, hooks={3: wo_add(0)})
            for i in range(2, 4):
                group(4, hooks={2: lambda: halve(3, i - 2, tiles(blk(4, 2))), 3: wo_add(i - 1)})
            pl.phase("ffn2_first")
            lo(4)
            modulation(20, 60, 80)
            then(scaled(2, "pre_ffn", 64, 1.0))
            halve(3, 2, tiles(blk(4, 2)))
            wo_add(3)()
            halve(3, 3, tiles(blk(4, 2)))

            def post_norm(k, a, sem):
                norm_rstd(k)
                for c in range(4):
                    for j in range(4 * c, 4 * c + 4):
                        ins = dve.scalar_tensor_tensor(out=O32[:, j], in0=O32[:, j], scalar=modA[:, a, j:j + 1],
                                                       in1=rstd[:], op0=ALU.mult, op1=ALU.mult)
                    then(ins)
                    q = slice(4 * c, 4 * c + 4)
                    dve.tensor_tensor(X[:, q], X[:, q], O32[:, q], ALU.add).then_inc(S(sem), 1)
            post_norm(3, 1, "x_mix")
            dve.wait_ge(S("x_mix"), 4)
            norm_rstd(4)
            norm_h(3, X, O32, modA[:, 2], 48)

            def square(n):
                i = n[0]
                dve.wait_ge(S("f2_relu"), n[1])
                o = act32[:, i * 1024:(i + 1) * 1024]
                dve.tensor_tensor(o, gtmp, gtmp, ALU.mult).then_inc(S("f2_act"), 1)

            def square_low(n, lo=yL, hi=yH):
                dve.wait_ge(S("f2_hi"), n)
                dve.tensor_tensor(lo[:, 0:8], tiles(act32), hi[:, 0:8].bitcast(F32), ALU.subtract)\
                   .then_inc(S("f2_lo"), 1)

            def add_down2(g, n, v):
                dve.wait_ge(S("w_used"), v)
                if not isinstance(n, int) or (n - 1) * 4 + g > 0:
                    dve.wait_ge(S("f2_sum"), (n - 1) * 4 + g)
                else:
                    dve.wait_ge(S("o_zero"), 1)
                o = O32[:, 4 * g:4 * g + 4]
                dve.tensor_tensor(o, o, tiles(acc[:, (PHASES["ffn2"][1] + g) % 2]), ALU.add).then_inc(S("f2_sum"), 1)

            def ffn2(n, begin, before, down):
                here = lambda: pl.v + pl.ov
                if down:
                    pl.phase("ffn2")
                lo(4 - begin)
                if before:
                    add_down2(3, n - 1, here() - 4)
                if down:
                    square_low(n)
                lo(4)
                lo(4)
                square((0, 2 * n + 1))
                lo(4)
                if down:
                    lo(4)
                square((1, 2 * n + 2))
                if down:
                    for g in range(3):
                        lo(4)
                        add_down2(g, n, here() - 4)

            ffn2(0, 4, False, False)
            ffn2(1, 0, False, True)
            with dve.Fori(0, 3) as i:
                pl.enter(i, 72, 64, 12, 1)
                for r in (2, 3):
                    ffn2(i * 2 + r, 0, True, True)
            pl.leave(3, 72, 64, 12, 1)
            modulation(24, 80, 96)
            then(scaled(3, "post_ffn", 80, 0.0))
            lo(4)
            square_low(8, hL, hH)
            add_down2(3, 7, pl.v - 4)
            lo(4)
            add_down2(0, 8, pl.v - 4)
            lo(4)
            add_down2(1, 8, pl.v - 4)
            lo(2)
            halve(5, 0, tiles(blk(4, 2)))
            lo(2)
            add_down2(2, 8, pl.v - 4)
            halve(5, 1, tiles(blk(4, 2)))
            halve(5, 2, tiles(blk(4, 2)))
            add_down2(3, 8, pl.v)
            halve(5, 3, tiles(blk(4, 2)))
            post_norm(5, 3, "x_done")


_RAW = ["w_in", "w_proj_a", "w_proj_b", "w_out", "w_ffn_in", "w_ffn_out", "w_ada_2", "w_in_2", "cmp_k_w1_2",
        "cmp_k_w2_2", "cmp_v_w1_2", "cmp_v_w2_2", "w_o_2", "w_up_2", "w_down_2"]


def kernel(**inputs):
    import concourse.bacc as bacc
    from concourse.bass_utils import run_bass_kernel_spmd

    x = {n: np.asarray(a) for n, a in inputs.items()}

    def columns(a):
        return a.reshape(-1, P).T

    consts, lmask = constants()
    arrays = {n: np.ascontiguousarray(x[n][0]) for n in _RAW}
    arrays["xT"] = np.ascontiguousarray(x["x"][0].T)
    arrays["rel_rev"] = np.ascontiguousarray(x["rel_bias"][0][:, ::-1])
    arrays["cols"] = np.ascontiguousarray(np.concatenate(
        [columns(x[n]) for n in ("norm_mix", "norm_ffn", "b_gate", "hgrn_lb_logits", "hgrn_out_gain", "q_gain",
                                 "k_gain", "c_2", "b_ada_2", "pre_norm_mix_2", "post_norm_mix_2", "pre_norm_ffn_2",
                                 "post_norm_ffn_2")] + [x["cmp_k_pos_2"][0].T, x["cmp_v_pos_2"][0].T], axis=1))
    arrays["consts"], arrays["lmask"] = consts, lmask
    nc = bacc.Bacc("TRN2", target_bir_lowering=False, num_devices=1)
    A = {n: nc.dram_tensor(f"in_{n}", a.shape, mybir.dt.from_np(a.dtype), kind="ExternalInput").ap()
         for n, a in arrays.items()}
    out = nc.dram_tensor("out_T", (D, T), F32, kind="ExternalOutput").ap()
    scratch = nc.dram_tensor("bias_ext", (H, EXT), F32, kind="Internal").ap()
    build(nc, A, out, scratch)
    r = run_bass_kernel_spmd(nc, [{f"in_{n}": a for n, a in arrays.items()}], core_ids=[0])
    return np.ascontiguousarray(r.results[0]["out_T"].T)[None]
```
